# Optimizing a Trainium2 kernel written in Bass

```python
import jax, jax.numpy as jnp
from jax import lax
import numpy as np

D_MODEL = 1024
BATCH = 1
SEQ = 1024
DEPTH = 1

CONV_DIM = D_MODEL
CONV_KERNEL = 31
POOL_DIM = D_MODEL
POOL_WINDOWS = (2, 4, 8, 16)
N_POOL_GROUPS = len(POOL_WINDOWS)
POOL_GROUP_DIM = POOL_DIM // N_POOL_GROUPS
POOL_OUT_GROUP_DIM = D_MODEL // N_POOL_GROUPS
D_FF = 2816
FFN_KERNEL = 3
IN_COLS = 2 * CONV_DIM + POOL_DIM + 2 * D_MODEL
EPS = 1e-6

kernel_name = "hybrid_gated_conformer_pool_block"

def rmsnorm(x, g):
    xf = x.astype(jnp.float32)
    y = xf * lax.rsqrt(jnp.mean(xf * xf, axis=-1, keepdims=True) + EPS)
    return (y * g.astype(jnp.float32)).astype(x.dtype)

def layernorm(x, g, b):
    xf = x.astype(jnp.float32)
    mu = jnp.mean(xf, axis=-1, keepdims=True)
    var = jnp.mean(jnp.square(xf - mu), axis=-1, keepdims=True)
    y = (xf - mu) * lax.rsqrt(var + EPS)
    return (y * g.astype(jnp.float32) + b.astype(jnp.float32)).astype(x.dtype)

def causal_dwconv(x, w, b):
    k, c = w.shape
    xp = jnp.pad(x, ((0, 0), (k - 1, 0), (0, 0)))
    y = lax.conv_general_dilated(
        xp, w[:, None, :].astype(x.dtype), window_strides=(1,), padding="VALID",
        dimension_numbers=("NWC", "WIO", "NWC"), feature_group_count=c)
    return y + b

def conformer_conv_branch(val, gate, dw_w, dw_b, ln_g, ln_b, w_out):
    u = val * jax.nn.sigmoid(gate)
    u = causal_dwconv(u, dw_w, dw_b)
    u = layernorm(u, ln_g, ln_b)
    u = jax.nn.silu(u)
    return jnp.einsum("bsc,cd->bsd", u, w_out)

def pool_branch(u, w_groups, scale):
    b, s, _ = u.shape
    uf = u.astype(jnp.float32).reshape(b, s, N_POOL_GROUPS, POOL_GROUP_DIM)
    cs = jnp.cumsum(uf, axis=1)
    pos1 = jnp.arange(1, s + 1, dtype=jnp.float32)[None, :, None]
    outs = []
    for g, w in enumerate(POOL_WINDOWS):
        c = cs[:, :, g]
        lag = jnp.pad(c[:, : s - w], ((0, 0), (w, 0), (0, 0)))
        cnt = jnp.minimum(pos1, float(w))
        outs.append((c - lag) / cnt - uf[:, :, g])
    pooled = jnp.stack(outs, axis=2).astype(u.dtype)
    y = jnp.einsum("bsgc,gcd->bsgd", pooled, w_groups).reshape(b, s, D_MODEL)
    return y * scale

def gdfn(h, w_up, dw_w, dw_b, w_down):
    u = jnp.einsum("bsd,df->bsf", h, w_up)
    u = causal_dwconv(u, dw_w, dw_b)
    a, g = jnp.split(u, 2, axis=-1)
    return jnp.einsum("bsf,fd->bsd", jax.nn.gelu(a) * g, w_down)

def setup_inputs(seed: int = 0) -> dict:
    key = jax.random.key(seed)
    ks = jax.random.split(key, 20)
    f32 = jnp.float32
    nrm = lambda k, shape: jax.random.normal(k, shape, f32)
    L, D = DEPTH, D_MODEL
    return {
        "x": nrm(ks[0], (BATCH, SEQ, D)),
        "w_in": nrm(ks[1], (L, D, IN_COLS)) * D ** -0.5,
        "b_in": nrm(ks[2], (L, IN_COLS)) * 0.02,
        "conv_dw_w": nrm(ks[3], (L, CONV_KERNEL, CONV_DIM)) * CONV_KERNEL ** -0.5,
        "conv_dw_b": nrm(ks[4], (L, CONV_DIM)) * 0.02,
        "conv_ln_g": 1.0 + 0.05 * nrm(ks[5], (L, CONV_DIM)),
        "conv_ln_b": 0.02 * nrm(ks[6], (L, CONV_DIM)),
        "conv_w_out": nrm(ks[7], (L, CONV_DIM, D)) * CONV_DIM ** -0.5,
        "pool_w": nrm(ks[8], (L, N_POOL_GROUPS, POOL_GROUP_DIM, POOL_OUT_GROUP_DIM)) * POOL_GROUP_DIM ** -0.5,
        "pool_scale": 1.0 + 0.05 * nrm(ks[9], (L, D)),
        "mix_w_out": nrm(ks[10], (L, D, D)) * D ** -0.5,
        "norm_mix": 1.0 + 0.05 * nrm(ks[11], (L, D)),
        "ffn_w_up": nrm(ks[12], (L, D, 2 * D_FF)) * D ** -0.5,
        "ffn_dw_w": nrm(ks[13], (L, FFN_KERNEL, 2 * D_FF)) * FFN_KERNEL ** -0.5,
        "ffn_dw_b": nrm(ks[14], (L, 2 * D_FF)) * 0.02,
        "ffn_w_down": nrm(ks[15], (L, D_FF, D)) * D_FF ** -0.5,
        "norm_ffn": 1.0 + 0.05 * nrm(ks[16], (L, D)),
        "norm_final": 1.0 + 0.05 * nrm(ks[17], (D,)),
    }

def reference(x, w_in, b_in, conv_dw_w, conv_dw_b, conv_ln_g, conv_ln_b, conv_w_out,
              pool_w, pool_scale, mix_w_out, norm_mix, ffn_w_up, ffn_dw_w, ffn_dw_b,
              ffn_w_down, norm_ffn, norm_final):
    c0 = CONV_DIM
    c1 = 2 * CONV_DIM
    c2 = c1 + POOL_DIM
    c3 = c2 + D_MODEL
    for l in range(DEPTH):
        h = rmsnorm(x, norm_mix[l])
        proj = jnp.einsum("bsd,dc->bsc", h, w_in[l]) + b_in[l]
        conv_val, conv_gate = proj[..., :c0], proj[..., c0:c1]
        pool_in = proj[..., c1:c2]
        gate_a = jax.nn.sigmoid(proj[..., c2:c3])
        gate_b = jax.nn.sigmoid(proj[..., c3:])
        ya = conformer_conv_branch(conv_val, conv_gate, conv_dw_w[l], conv_dw_b[l],
                                   conv_ln_g[l], conv_ln_b[l], conv_w_out[l])
        yb = pool_branch(pool_in, pool_w[l], pool_scale[l])
        merged = gate_a * ya + gate_b * yb
        x = x + jnp.einsum("bsd,de->bse", merged, mix_w_out[l])
        h = rmsnorm(x, norm_ffn[l])
        x = x + gdfn(h, ffn_w_up[l], ffn_dw_w[l], ffn_dw_b[l], ffn_w_down[l])
    return rmsnorm(x, norm_final)


_drawn_inputs = setup_inputs


def setup_inputs(seed=0):
    import zlib

    import numpy as np

    out = dict(_drawn_inputs(seed))
    spreads = {}
    factors = {'b_in': 6.445,
     'conv_dw_b': 4.413,
     'conv_ln_g': 2.858,
     'conv_ln_b': 8.0,
     'ffn_dw_b': 4.066,
     'pool_scale': 3.492,
     'norm_ffn': 2.711}
    for name, (base, spread) in spreads.items():
        noise = np.random.default_rng([zlib.crc32(name.encode()), seed]).standard_normal(out[name].shape)
        drawn = base * np.exp(spread * noise) if base else spread * noise
        out[name] = __import__('jax').numpy.asarray(drawn.astype(out[name].dtype))
    for name, factor in factors.items():
        out[name] = (out[name] * factor).astype(out[name].dtype)
    return out
```

```python
EPS = 1e-6
P = 128
SEQ = 1024
HALF = SEQ // 2
DM = 1024
KT = DM // P
TAPS = 31
PAD = TAPS - 1
WINDOWS = (2, 4, 8, 16)
NG = len(WINDOWS)
WPAD = max(WINDOWS)
D_FF = 2816
FT = D_FF // P
CH = 8 * P
CHUNK_PAIRS = 2
STEPS = FT // CHUNK_PAIRS

_cols = {}
_n = 0
for _name, _w in (("b_in", 5 * KT), ("conv_w", KT * TAPS), ("conv_b", KT), ("ln_g", KT), ("ln_b", KT),
                  ("scale", KT), ("norm_mix", KT), ("norm_ffn", KT), ("norm_final", KT),
                  ("ffn_w", 2 * FT * 3), ("ffn_b", 2 * FT), ("edge", NG * WPAD)):
    _cols[_name] = _n
    _n += _w
NPAR = _n

N_POOL = 0
N_CONV = N_POOL + KT
N_GATE_A = N_CONV + 3 * KT
N_OUT = N_GATE_A + KT
N_MIX = N_OUT + KT
N_FFN = N_MIX + KT
UPC = 2 * CHUNK_PAIRS
DNC = 2
NCHUNKS = N_FFN + STEPS * (UPC + DNC)


def build(nc, xT, wstream, pool_w, params, outT):
    import concourse.bass as bass
    from concourse import mybir
    from contextlib import ExitStack

    f32, f32r = mybir.dt.float32, mybir.dt.float32r
    ACT = mybir.ActivationFunctionType
    ALU = mybir.AluOpType

    ctx = ExitStack()
    with ctx:
        def sb(name, cols, dt=f32):
            return ctx.enter_context(nc.sbuf_tensor(name, [P, cols], dt))

        def two_views(name_f32, name_f32r, cols):
            with nc.sbuf_tensor(name_f32, [P, cols], f32) as plain:
                pass
            return plain, sb(name_f32r, cols, f32r)

        def sem(name):
            return ctx.enter_context(nc.semaphore(name))

        TS = KT * SEQ
        h_hi, h_lo = sb("h_hi", TS, f32r), sb("h_lo", TS, f32r)
        res = sb("res", TS)
        cv, cv_r = two_views("cv", "cv_r", TS)
        ga, ga_r = two_views("ga", "ga_r", TS)
        raw = sb("raw", 2 * CH)
        w_hi, w_lo = sb("w_hi", 2 * CH, f32r), sb("w_lo", 2 * CH, f32r)
        tmp = sb("tmp", 4 * SEQ)
        par = sb("par", NPAR)
        ones = sb("ones", P)
        ident = sb("ident", P)
        small = sb("small", 64)
        ps = ctx.enter_context(nc.psum_tensor("ps", [P, 4 * SEQ], f32))

        def slot(n, a=0, b=SEQ):
            return ps[:, n * SEQ + a:n * SEQ + b]

        def tile(t, i, a=0, b=SEQ):
            return t[:, bass.ds(i * SEQ + a, b - a)]

        def par1(name, i):
            return par[:, bass.ds(i + _cols[name], 1)]

        GL = tmp[:, 0:PAD + SEQ]
        csum = tmp[:, PAD + SEQ:PAD + 2 * SEQ]
        ln_sq = [tmp[:, 0:SEQ], tmp[:, 2080:2080 + SEQ]]
        ln_diag = csum
        nsq = [tmp[:, i * HALF:(i + 1) * HALF] for i in range(2)]
        nt = [tmp[:, (2 + i) * HALF:(3 + i) * HALF] for i in range(2)]
        ndiag = tmp[:, 4 * HALF:5 * HALF]
        acc_a = [tmp[:, i * SEQ:(i + 1) * SEQ] for i in range(2)]
        acc_b = [tmp[:, (2 + i) * SEQ:(3 + i) * SEQ] for i in range(2)]
        XW = WPAD + SEQ
        px = [cv[:, i * XW:(i + 1) * XW] for i in range(2)]
        pst = [cv[:, (2 + i) * XW:(3 + i) * XW] for i in range(2)]
        pw_raw = cv[:, 4 * XW:4 * XW + 2 * CH]
        pp_hi = [ga_r[:, i * SEQ:(i + 1) * SEQ] for i in range(2)]
        pp_lo = [ga_r[:, (2 + i) * SEQ:(3 + i) * SEQ] for i in range(2)]
        pw_hi, pw_lo = ga_r[:, 4 * SEQ:6 * SEQ], ga_r[:, 6 * SEQ:8 * SEQ]

        par_loaded, pw_loaded, xre_loaded, out_stored = (sem(n) for n in ("par_loaded", "pw_loaded", "xre_loaded", "out_stored"))
        x_loaded = [sem(f"x_loaded{h}") for h in range(2)]
        raw_loaded = [sem(f"raw_loaded{s}") for s in range(2)]
        split_go, w_hi_done, w_split, w_used = sem("split_go"), sem("w_hi_done"), sem("w_split"), sem("w_used")
        consts = sem("consts")
        names = ("sq", "sqmm", "ss", "std", "rinv", "diag", "bc", "val", "hi", "lo")
        norm_sem = {(tag, h): {n: sem(f"{tag}{h}_{n}") for n in names}
                    for tag in ("n1", "n2", "nf") for h in range(2)}
        pw_hi_done, pw_lo_done = sem("pw_hi_done"), sem("pw_lo_done")
        p_in, p_dve, p_hi, p_lo, pool_mm, yb_done = (sem(n) for n in ("p_in", "p_dve", "p_hi", "p_lo", "pool_mm", "yb_done"))
        sig_gate, sig_gb, glu_done, conv_step, cv_done, cs_done, gb_done = (
            sem(n) for n in ("sig_gate", "sig_gb", "glu_done", "conv_step", "cv_done", "cs_done", "gb_done"))
        pads = sem("pads")
        sa_done = sem("sa_done")
        ln_mean, ln_d, ln_sqd, ln_sqmm, ln_ss, ln_std, ln_rinv, ln_dg, ln_bc, ln_n, ln_z, z_hi, z_lo = (
            sem(n) for n in ("ln_mean", "ln_d", "ln_sqd", "ln_sqmm", "ln_ss", "ln_std", "ln_rinv", "ln_dg",
                             "ln_bc", "ln_n", "ln_z", "z_hi", "z_lo"))
        co_a, co_m, co_hi, co_lo = (sem(n) for n in ("co_a", "co_m", "co_hi", "co_lo"))
        x1_done = sem("x1_done")
        f_acca, f_accb, f_ca1, f_ca, f_cb1, f_cb, f_gelu, f_g, f_hi, f_lo, dn_mm, dn_ev = (
            sem(n) for n in ("f_acca", "f_accb", "f_ca1", "f_ca", "f_cb1", "f_cb", "f_gelu", "f_g", "f_hi", "f_lo", "dn_mm", "dn_ev"))

        block = ctx.enter_context(nc.Block())

        def wait(eng, s, v):
            if not (isinstance(v, int) and v <= 0):
                eng.wait_ge(s, v)

        @block.sync
        def _(sp):
            sp.dma_start(par[:, :], params).then_inc(par_loaded, 16)
            for h in range(2):
                sp.dma_start(res[:, :].rearrange("p (k n) -> p k n", k=KT)[:, :, h * HALF:(h + 1) * HALF],
                             xT.rearrange("(k p) n -> p k n", p=P)[:, :, h * HALF:(h + 1) * HALF]).then_inc(x_loaded[h], 16)
                if h == 0:
                    for s in range(2):
                        sp.dma_start(raw[:, s * CH:(s + 1) * CH], wstream[s * P:(s + 1) * P, :]).then_inc(raw_loaded[s], 16)
            sp.dma_start(pw_raw, pool_w).then_inc(pw_loaded, 16)
            with sp.Fori(1, NCHUNKS // 2) as i:
                for s in range(2):
                    sp.wait_ge(w_split, 2 * i + s - 1)
                    sp.dma_start(raw[:, s * CH:(s + 1) * CH],
                                 wstream[bass.ds((2 * i + s) * P, P), :]).then_inc(raw_loaded[s], 16)
            for h in range(2):
                for q in range(2):
                    sp.wait_ge(norm_sem["nf", h]["val"], 4 * (q + 1))
                    sp.dma_start(
                        outT.rearrange("(k p) n -> p k n", p=P)[:, 4 * q:4 * q + 4, h * HALF:(h + 1) * HALF],
                        res[:, :].rearrange("p (k n) -> p k n", k=KT)[:, 4 * q:4 * q + 4, h * HALF:(h + 1) * HALF],
                    ).then_inc(out_stored, 16)
            sp.wait_ge(out_stored, 64)

        @block.gpsimd
        def _(pool):
            pool.memset(ones[:, :], 1.0).then_inc(consts, 1)
            pool.memset(small[:, 60:61], EPS).then_inc(consts, 1)
            pool.memset(ident[:, :], 0.0).then_inc(consts, 1)
            pool.wait_ge(consts, 3)
            pool.affine_select(out=ident[:, :], in_=ident[:, :], compare_op=ALU.not_equal, fill=1.0,
                               base=0, pattern=[[-1, P]], channel_multiplier=1).then_inc(consts, 1)

            def split(n, s, i):
                pool.wait_ge(raw_loaded[s], 16 * (i + 1))
                wait(pool, w_used, n - 1)
                pool.sem_inc(split_go, 1)
                r, hi, lo = (t[:, s * CH:(s + 1) * CH] for t in (raw, w_hi, w_lo))
                pool.tensor_copy(hi, r).then_inc(w_hi_done, 1)
                pool.wait_ge(w_hi_done, n + 1)
                pool.tensor_tensor(lo, r, hi.bitcast(f32), ALU.subtract).then_inc(w_split, 1)

            for s in range(2):
                split(s, s, 0)
            with pool.Fori(1, NCHUNKS // 2) as i:
                for s in range(2):
                    split(2 * i + s, s, i)

        @block.scalar
        def _(act):
            eps = small[:, 60:61]

            def norm(tag, h, ready, ready_val, split):
                z = norm_sem[tag, h]
                for k in range(KT):
                    act.wait_ge(ready, ready_val(k))
                    if k >= 2:
                        act.wait_ge(z["sqmm"], k - 1)
                    act.activation(nsq[k % 2], tile(res, k, h * HALF, (h + 1) * HALF), ACT.Square).then_inc(z["sq"], 1)
                act.wait_ge(z["ss"], 1)
                act.activation(small[:, 8 * h:8 * h + 4], slot(2 + h, 0, 4), ACT.Sqrt, bias=eps, scale=1.0 / DM).then_inc(z["std"], 1)

            def norm_hi(tag, h):
                z = norm_sem[tag, h]
                for k in range(KT):
                    act.wait_ge(z["val"], k + 1)
                    act.activation(tile(h_hi, k, h * HALF, (h + 1) * HALF), nt[k % 2], ACT.Copy).then_inc(z["hi"], 1)

            act.wait_ge(consts, 4)
            norm("n1", 0, x_loaded[0], lambda k: 16, True)
            act.wait_ge(par_loaded, 16)
            norm_hi("n1", 0)
            norm("n1", 1, x_loaded[1], lambda k: 16, True)
            norm_hi("n1", 1)
            act.wait_ge(pw_loaded, 16)
            act.activation(pw_hi, pw_raw, ACT.Copy).then_inc(pw_hi_done, 1)

            def pool_in(g):
                for j in range(2):
                    act.wait_ge(w_used, N_POOL + 2 * g + j + 1)
                    wait(act, p_lo, 2 * g)
                    act.activation(px[j][:, WPAD:], slot(j), ACT.Identity, bias=par1("b_in", 2 * KT + 2 * g + j)).then_inc(p_in, 1)

            def pool_hi(g):
                for j in range(2):
                    act.wait_ge(p_dve, 2 * g + j + 1)
                    wait(act, pool_mm, 2 * g)
                    act.activation(pp_hi[j], px[j][:, WPAD:], ACT.Copy).then_inc(p_hi, 1)

            def pool_out(g):
                for m in range(2):
                    act.wait_ge(pool_mm, 2 * g + m + 1)
                    act.activation(tile(res, 2 * g + m), slot(2 + m), ACT.Copy, scale=par1("scale", 2 * g + m)).then_inc(yb_done, 1)

            pool_in(0)
            pool_hi(0)
            with act.Fori(1, NG) as g:
                pool_in(g)
                pool_out(g - 1)
                pool_hi(g)

            def gates(c, first=False):
                act.wait_ge(w_used, N_CONV + 3 * c + 2)
                if first:
                    act.wait_ge(p_lo, 2 * NG)
                act.activation(tile(cv, c), slot(1), ACT.Sigmoid, bias=par1("b_in", KT + c)).then_inc(sig_gate, 1)
                if first:
                    pool_out(NG - 1)
                act.wait_ge(w_used, N_CONV + 3 * c + 3)
                act.activation(slot(2), slot(2), ACT.Sigmoid, bias=par1("b_in", 4 * KT + c)).then_inc(sig_gb, 1)

            gates(0, True)
            with act.Fori(1, KT) as c:
                gates(c)

            def gate_a(i):
                for j in range(2):
                    act.wait_ge(w_used, N_GATE_A + 2 * i + j + 1)
                    act.activation(tile(ga, 2 * i + j), slot(j), ACT.Sigmoid, bias=par1("b_in", 3 * KT + 2 * i + j)).then_inc(sa_done, 1)

            act.wait_ge(pool_mm, 2 * NG)
            with act.Fori(0, KT // 2 - 1) as i:
                gate_a(i)

            for c in range(KT):
                act.wait_ge(ln_d, c + 1)
                if c >= 2:
                    act.wait_ge(ln_sqmm, c - 1)
                act.activation(ln_sq[c % 2], tile(cv, c), ACT.Square).then_inc(ln_sqd, 1)
            gate_a(KT // 2 - 1)
            act.wait_ge(ln_ss, 1)
            act.activation(small[:, 16:16 + KT], slot(3, 0, KT), ACT.Sqrt, bias=eps, scale=1.0 / DM).then_inc(ln_std, 1)
            with act.Fori(0, KT) as c:
                act.wait_ge(ln_n, c + 1)
                act.activation(tile(cv, c), tile(cv, c), ACT.Silu, bias=par1("ln_b", c), scale=par1("ln_g", c)).then_inc(ln_z, 1)
                act.wait_ge(w_used, N_OUT)
                act.wait_ge(ln_z, c + 1)
                act.activation(tile(h_hi, c), tile(cv, c), ACT.Copy).then_inc(z_hi, 1)

            act.wait_ge(z_lo, KT)
            xr = xT.rearrange("(k p) n -> p k n", p=P)
            with act.Fori(0, KT // 2) as i:
                for j in range(2):
                    act.wait_ge(co_m, 2 * i + j + 1)
                    act.activation(tile(cv_r, 2 * i + j), tile(res, 2 * i + j), ACT.Copy).then_inc(co_hi, 1)
                act.wait_ge(co_lo, 2 * i + 2)
                act.dma_start(res[:, bass.ds(2 * i * SEQ, 2 * SEQ)].rearrange("p (k n) -> p k n", k=2),
                              xr[:, bass.ds(2 * i, 2), :]).then_inc(xre_loaded, 16)

            for h in range(2):
                norm("n2", h, x1_done, lambda k: k + 1, True)
                norm_hi("n2", h)

            def up(p, s, gs, n, dn_need):
                act.wait_ge(w_used, n + 1)
                wait(act, f_g, p - 1)
                act.activation(acc_a[s], slot(2 * s), ACT.Identity, bias=par1("ffn_b", p), scale=par1("ffn_w", p * 3 + 2)).then_inc(f_acca, 1)
                act.wait_ge(f_ca, p + 1)
                act.activation(acc_a[s], acc_a[s], ACT.Gelu_apprx_tanh).then_inc(f_gelu, 1)
                act.wait_ge(w_used, n + 2)
                wait(act, f_lo, p - 1)
                act.activation(acc_b[s], slot(2 * s + 1), ACT.Identity, bias=par1("ffn_b", p + FT), scale=par1("ffn_w", (p + FT) * 3 + 2)).then_inc(f_accb, 1)
                act.wait_ge(f_g, p + 1)
                if dn_need is not None:
                    act.wait_ge(w_used, dn_need)
                act.activation(tile(cv_r, gs), acc_b[s], ACT.Copy).then_inc(f_hi, 1)

            up(0, 0, 0, N_FFN, None)
            up(1, 1, 1, N_FFN + 2, None)

            def ffn(i):
                n = N_FFN + UPC + 12 * i
                for s in range(2):
                    up(4 * i + 2 + s, s, 2 + s, n + 2 * s, None if isinstance(i, int) else n)
                for s in range(2):
                    up(4 * i + 4 + s, s, s, n + 6 + 2 * s, n + 6)
            ffn(0)
            with act.Fori(1, STEPS // 2) as i:
                ffn(i)

            for h in range(2):
                norm("nf", h, dn_ev, lambda k: 8 * (STEPS - 1) + k + 1, False)

        @block.vector
        def _(dve):
            def norm_stat(tag, h):
                z = norm_sem[tag, h]
                dve.wait_ge(z["std"], 1)
                dve.reciprocal(small[:, 8 * h + 4:8 * h + 8], small[:, 8 * h:8 * h + 4]).then_inc(z["rinv"], 1)
                dve.wait_ge(z["rinv"], 1)
                if h:
                    dve.wait_ge(norm_sem[tag, 0]["bc"], 1)
                for j in range(4):
                    dve.tensor_scalar(ndiag[:, j * P:(j + 1) * P], ident[:, :], small[:, 8 * h + 4 + j:8 * h + 5 + j], None,
                                      ALU.mult).then_inc(z["diag"], 1)

            def norm(tag, h, gain):
                z = norm_sem[tag, h]
                norm_stat(tag, h)
                dve.wait_ge(z["bc"], 1)
                r = (h * HALF, (h + 1) * HALF)
                for k in range(KT):
                    if k >= 2:
                        dve.wait_ge(z["lo"], k - 1)
                    dve.scalar_tensor_tensor(out=nt[k % 2], in0=tile(res, k, *r), scalar=par1(gain, k),
                                             in1=slot(2 + h, HALF, SEQ), op0=ALU.mult, op1=ALU.mult).then_inc(z["val"], 1)
                    if k:
                        low(tag, h, k - 1)
                low(tag, h, KT - 1)

            def low(tag, h, k):
                z = norm_sem[tag, h]
                r = (h * HALF, (h + 1) * HALF)
                dve.wait_ge(z["hi"], k + 1)
                dve.tensor_tensor(tile(h_lo, k, *r), nt[k % 2], tile(h_hi, k, *r).bitcast(f32), ALU.subtract).then_inc(z["lo"], 1)

            dve.wait_ge(consts, 4)
            dve.wait_ge(par_loaded, 16)
            for h in range(2):
                if h:
                    dve.wait_ge(norm_sem["n1", 0]["lo"], KT)
                norm("n1", h, "norm_mix")
            dve.wait_ge(norm_sem["n1", 1]["lo"], KT)
            for t in px + pst:
                dve.memset(t[:, 0:WPAD], 0.0).then_inc(pads, 1)
            dve.memset(GL[:, 0:PAD], 0.0).then_inc(pads, 1)
            dve.memset(csum, 0.0).then_inc(pads, 1)
            dve.wait_ge(pw_hi_done, 1)
            dve.tensor_tensor(pw_lo, pw_raw, pw_hi.bitcast(f32), ALU.subtract).then_inc(pw_lo_done, 1)
            dve.wait_ge(pads, 6)

            sums = [0]

            def added(ins):
                sums[0] += 1
                ins.then_inc(pads, 1)
                dve.wait_ge(pads, 6 + sums[0])

            for g, w in enumerate(WINDOWS):
                for j in range(2):
                    dve.wait_ge(p_in, 2 * g + j + 1)
                    src, d, n = px[j], 1, 0
                    while d < w:
                        added(dve.tensor_tensor(pst[n][:, WPAD:], src[:, WPAD:], src[:, WPAD - d:WPAD - d + SEQ], ALU.add))
                        src, d, n = pst[n], 2 * d, 1 - n
                    e = _cols["edge"] + g * WPAD
                    added(dve.tensor_tensor(src[:, WPAD:2 * WPAD], src[:, WPAD:2 * WPAD], par[:, e:e + WPAD], ALU.mult))
                    dve.scalar_tensor_tensor(out=px[j][:, WPAD:], in0=src[:, WPAD:], scalar=1.0 / w, in1=px[j][:, WPAD:],
                                             op0=ALU.mult, op1=ALU.subtract).then_inc(p_dve, 1)
                    dve.wait_ge(p_dve, 2 * g + j + 1)
                for j in range(2):
                    dve.wait_ge(p_hi, 2 * g + j + 1)
                    if g:
                        dve.wait_ge(pool_mm, 2 * g)
                    dve.tensor_tensor(pp_lo[j], px[j][:, WPAD:], pp_hi[j].bitcast(f32), ALU.subtract).then_inc(p_lo, 1)

            def conv(c, first=False):
                dve.wait_ge(sig_gate, c + 1)
                wait(dve, cs_done, c)
                dve.scalar_tensor_tensor(out=GL[:, PAD:], in0=slot(0), scalar=par1("b_in", c), in1=tile(cv, c),
                                         op0=ALU.add, op1=ALU.mult).then_inc(glu_done, 1)
                dve.wait_ge(glu_done, c + 1)
                if first:
                    dve.wait_ge(yb_done, 2 * NG)
                step = 30 * c
                dve.tensor_scalar(slot(3), GL[:, PAD:], par1("conv_w", c * TAPS + PAD), par1("conv_b", c),
                                  ALU.mult, ALU.add).then_inc(conv_step, 1)
                for t in range(PAD - 1):
                    dve.wait_ge(conv_step, step + t + 1)
                    dve.scalar_tensor_tensor(out=slot(3), in0=GL[:, t:t + SEQ], scalar=par1("conv_w", c * TAPS + t),
                                             in1=slot(3), op0=ALU.mult, op1=ALU.add).then_inc(conv_step, 1)
                    if t == 16:
                        dve.wait_ge(sig_gb, c + 1)
                        dve.tensor_tensor(tile(res, c), slot(2), tile(res, c), ALU.mult).then_inc(gb_done, 1)
                dve.wait_ge(conv_step, step + PAD)
                dve.scalar_tensor_tensor(out=tile(cv, c), in0=GL[:, PAD - 1:PAD - 1 + SEQ], scalar=par1("conv_w", c * TAPS + PAD - 1),
                                         in1=slot(3), op0=ALU.mult, op1=ALU.add).then_inc(cv_done, 1)
                dve.wait_ge(cv_done, c + 1)
                dve.tensor_tensor(csum, csum, tile(cv, c), ALU.add).then_inc(cs_done, 1)

            conv(0, True)
            with dve.Fori(1, KT) as c:
                conv(c)

            dve.wait_ge(ln_mean, 1)
            with dve.Fori(0, KT) as c:
                dve.scalar_tensor_tensor(out=tile(cv, c), in0=slot(2), scalar=-1.0 / DM, in1=tile(cv, c),
                                         op0=ALU.mult, op1=ALU.add).then_inc(ln_d, 1)
            dve.wait_ge(ln_std, 1)
            dve.reciprocal(small[:, 24:24 + KT], small[:, 16:16 + KT]).then_inc(ln_rinv, 1)
            dve.wait_ge(ln_rinv, 1)
            for j in range(KT):
                dve.tensor_scalar(ln_diag[:, j * P:(j + 1) * P], ident[:, :], small[:, 24 + j:25 + j], None, ALU.mult).then_inc(ln_dg, 1)
            dve.wait_ge(ln_bc, 1)
            dve.wait_ge(ln_d, KT)
            with dve.Fori(0, KT) as c:
                dve.tensor_tensor(tile(cv, c), slot(2), tile(cv, c), ALU.mult).then_inc(ln_n, 1)
            with dve.Fori(0, KT) as c:
                dve.wait_ge(z_hi, c + 1)
                dve.tensor_tensor(tile(h_lo, c), tile(cv, c), tile(h_hi, c).bitcast(f32), ALU.subtract).then_inc(z_lo, 1)

            dve.wait_ge(sa_done, KT)
            dve.wait_ge(gb_done, KT)
            with dve.Fori(0, KT // 2) as i:
                for j in range(2):
                    m = 2 * i + j
                    dve.wait_ge(w_used, N_OUT + m + 1)
                    dve.tensor_tensor(tile(ga, m), slot(j), tile(ga, m), ALU.mult).then_inc(co_a, 1)
                    dve.wait_ge(co_a, m + 1)
                    dve.tensor_tensor(tile(res, m), tile(ga, m), tile(res, m), ALU.add).then_inc(co_m, 1)
                    dve.wait_ge(co_hi, m + 1)
                    dve.tensor_tensor(tile(ga_r, m), tile(res, m), tile(cv_r, m).bitcast(f32), ALU.subtract).then_inc(co_lo, 1)

            dve.wait_ge(xre_loaded, 16 * (KT // 2))
            with dve.Fori(0, KT // 2) as i:
                for j in range(2):
                    dve.wait_ge(w_used, N_MIX + 2 * i + j + 1)
                    dve.tensor_tensor(tile(res, 2 * i + j), slot(j), tile(res, 2 * i + j), ALU.add).then_inc(x1_done, 1)
            dve.wait_ge(x1_done, KT)
            for h in range(2):
                if h:
                    dve.wait_ge(norm_sem["n2", 0]["lo"], KT)
                norm("n2", h, "norm_ffn")

            def up(p, s, gs):
                for f, acc, started, first_tap, done, n in ((p, acc_a[s], f_acca, f_ca1, f_ca, 2 * s),
                                                            (p + FT, acc_b[s], f_accb, f_cb1, f_cb, 2 * s + 1)):
                    dve.wait_ge(started, p + 1)
                    for d, s_done in ((1, first_tap), (2, done)):
                        dve.scalar_tensor_tensor(out=acc[:, d:], in0=slot(n, 0, SEQ - d), scalar=par1("ffn_w", f * 3 + 2 - d),
                                                 in1=acc[:, d:], op0=ALU.mult, op1=ALU.add).then_inc(s_done, 1)
                        if d == 1:
                            dve.wait_ge(s_done, p + 1)
                dve.wait_ge(f_gelu, p + 1)
                dve.wait_ge(f_cb, p + 1)
                dve.tensor_tensor(acc_b[s], acc_a[s], acc_b[s], ALU.mult).then_inc(f_g, 1)
                dve.wait_ge(f_hi, p + 1)
                dve.tensor_tensor(tile(ga_r, gs), acc_b[s], tile(cv_r, gs).bitcast(f32), ALU.subtract).then_inc(f_lo, 1)

            def down(q, n):
                for m in range(KT):
                    if m % 4 == 3:
                        dve.wait_ge(w_used, n + m // 4 + 1)
                    else:
                        dve.wait_ge(dn_mm, 6 * q + m - m // 4 + 1)
                    wait(dve, dn_ev, 8 * q + m)
                    dve.tensor_tensor(tile(res, m), slot(m % 4), tile(res, m), ALU.add).then_inc(dn_ev, 1)

            dve.wait_ge(norm_sem["n2", 1]["lo"], KT)
            for s in range(2):
                up(s, s, s)

            def ffn(i):
                n = N_FFN + UPC + 12 * i
                for s in range(2):
                    up(4 * i + 2 + s, s, 2 + s)
                down(2 * i, n + 4)
                for s in range(2):
                    up(4 * i + 4 + s, s, s)
                down(2 * i + 1, n + 10)
            ffn(0)
            with dve.Fori(1, STEPS // 2) as i:
                ffn(i)
            down(STEPS - 1, NCHUNKS - 2)

            dve.wait_ge(dn_ev, 8 * STEPS)
            for h in range(2):
                z = norm_sem["nf", h]
                norm_stat("nf", h)
                dve.wait_ge(z["bc"], 1)
                for k in range(KT):
                    t = tile(res, k, h * HALF, (h + 1) * HALF)
                    dve.scalar_tensor_tensor(out=t, in0=t, scalar=par1("norm_final", k), in1=slot(2 + h, HALF, SEQ),
                                             op0=ALU.mult, op1=ALU.mult).then_inc(z["val"], 1)

        @block.tensor
        def _(pe):
            def three(out, a_hi, a_lo, b_hi, b_lo, start, stop):
                nc.tensor.matmul(out, a_hi, b_lo, start=start, stop=False)
                nc.tensor.matmul(out, a_lo, b_hi, start=False, stop=False)
                return nc.tensor.matmul(out, a_hi, b_hi, start=False, stop=stop)

            def project(n, s, dst, mov_hi, mov_lo, half_ready=None):
                pe.wait_ge(w_split, n + 1)
                for h in range(2):
                    if half_ready:
                        pe.wait_ge(half_ready[h], KT)
                    for k in range(KT):
                        c = s * CH + k * P
                        last = three(slot(dst, h * HALF, (h + 1) * HALF), w_hi[:, c:c + P], w_lo[:, c:c + P],
                                     tile(mov_hi, k, h * HALF, (h + 1) * HALF), tile(mov_lo, k, h * HALF, (h + 1) * HALF),
                                     k == 0, k == KT - 1)
                last.then_inc(w_used, 1)

            def norm(tag, h):
                z = norm_sem[tag, h]
                for k in range(KT):
                    pe.wait_ge(z["sq"], k + 1)
                    for j in range(4):
                        last = nc.tensor.matmul(slot(2 + h, j, j + 1), nsq[k % 2][:, j * P:(j + 1) * P], ones[:, 0:1],
                                                start=(k == 0 and j == 0), stop=(k == KT - 1), skip_group_check=True)
                    last.then_inc(z["sqmm"] if k < KT - 1 else z["ss"], 1)
                pe.wait_ge(z["diag"], 4)
                nc.tensor.matmul(slot(2 + h, HALF, SEQ), ones[:, :], ndiag, start=True, stop=True).then_inc(z["bc"], 1)

            pe.wait_ge(consts, 4)
            for h in range(2):
                norm("n1", h)

            n1_ready = [norm_sem["n1", h]["lo"] for h in range(2)]

            def pool_project(g):
                for j in range(2):
                    wait(pe, p_in, 2 * g)
                    project(N_POOL + 2 * g + j, j, j, h_hi, h_lo, n1_ready)

            def pool_map(g, gw):
                pe.wait_ge(p_lo, 2 * (g + 1))
                wait(pe, yb_done, 2 * g)
                for m in range(2):
                    for h in range(2):
                        for k in range(2):
                            last = three(slot(2 + m, h * HALF, (h + 1) * HALF), gw(pw_hi, k, m), gw(pw_lo, k, m),
                                         pp_hi[k][:, h * HALF:(h + 1) * HALF], pp_lo[k][:, h * HALF:(h + 1) * HALF],
                                         k == 0, k == 1)
                    last.then_inc(pool_mm, 1)

            def static_w(g):
                return lambda t, k, m: t[:, g * 4 * P + (2 * k + m) * P:g * 4 * P + (2 * k + m + 1) * P]

            pool_project(0)
            pe.wait_ge(pw_lo_done, 1)
            for g in range(1, NG):
                pool_project(g)
                pool_map(g - 1, static_w(g - 1))

            def conv_project(c, s, between=None):
                wait(pe, glu_done, c)
                project(N_CONV + 3 * c, s, 0, h_hi, h_lo)
                wait(pe, sig_gate, c)
                project(N_CONV + 3 * c + 1, 1 - s, 1, h_hi, h_lo)
                if between:
                    between()
                wait(pe, gb_done, c)
                project(N_CONV + 3 * c + 2, s, 2, h_hi, h_lo)

            def last_group():
                pool_map(NG - 1, static_w(NG - 1))
                pe.wait_ge(yb_done, 2 * NG)

            pe.wait_ge(p_in, 2 * NG)
            conv_project(0, 0, last_group)
            conv_project(1, 1)
            with pe.Fori(1, KT // 2) as i:
                for j in range(2):
                    conv_project(2 * i + j, j)

            pe.wait_ge(glu_done, KT)
            pe.wait_ge(sig_gate, KT)

            def gate_a(i, first=False):
                for j in range(2):
                    if not first:
                        wait(pe, sa_done, 2 * i + j - 1)
                    project(N_GATE_A + 2 * i + j, j, j, h_hi, h_lo)
            gate_a(0, True)
            with pe.Fori(1, KT // 2 - 1) as i:
                gate_a(i)
            pe.wait_ge(cs_done, KT)
            pe.wait_ge(gb_done, KT)
            for h in range(2):
                last = nc.tensor.matmul(slot(2, h * HALF, (h + 1) * HALF), ones[:, :], csum[:, h * HALF:(h + 1) * HALF],
                                        start=True, stop=True)
            last.then_inc(ln_mean, 1)
            gate_a(KT // 2 - 1)
            for c in range(KT):
                pe.wait_ge(ln_sqd, c + 1)
                for j in range(KT):
                    last = nc.tensor.matmul(slot(3, j, j + 1), ln_sq[c % 2][:, j * P:(j + 1) * P], ones[:, 0:1],
                                            start=(c == 0 and j == 0), stop=(c == KT - 1), skip_group_check=True)
                last.then_inc(ln_sqmm if c < KT - 1 else ln_ss, 1)
            pe.wait_ge(ln_dg, KT)
            for h in range(2):
                last = nc.tensor.matmul(slot(2, h * HALF, (h + 1) * HALF), ones[:, :], ln_diag[:, h * HALF:(h + 1) * HALF],
                                        start=True, stop=True)
            last.then_inc(ln_bc, 1)

            pe.wait_ge(z_lo, KT)
            pe.wait_ge(sa_done, KT)

            def out_project(i, first=False):
                for j in range(2):
                    if not first:
                        wait(pe, co_a, 2 * i + j - 1)
                    project(N_OUT + 2 * i + j, j, j, h_hi, h_lo)
            out_project(0, True)
            with pe.Fori(1, KT // 2) as i:
                out_project(i)

            pe.wait_ge(co_lo, KT)

            def mix_project(i, first=False):
                for j in range(2):
                    if not first:
                        wait(pe, x1_done, 2 * i + j - 1)
                    project(N_MIX + 2 * i + j, j, j, cv_r, ga_r)
            mix_project(0, True)
            with pe.Fori(1, KT // 2) as i:
                mix_project(i)
            for h in range(2):
                norm("n2", h)
            n2_ready = [norm_sem["n2", h]["lo"] for h in range(2)]

            def up(p, s, n, dn):
                wait(pe, f_cb, p - 1)
                for j in range(2):
                    if dn is not None:
                        pe.wait_ge(dn_ev, dn + 2 * s + j)
                    project(n + j, j, 2 * s + j, h_hi, h_lo, n2_ready if dn is None else None)

            def down(q, n, gs):
                pe.wait_ge(f_lo, 2 * q + 2)
                for m in range(KT):
                    if m % 4 == 0:
                        pe.wait_ge(w_split, n + m // 4 + 1)
                    if m < 4:
                        pe.wait_ge(f_cb, 2 * q + 3 + m // 2)
                    else:
                        pe.wait_ge(dn_ev, 8 * q + m - 3)
                    for h in range(2):
                        for k in range(2):
                            c = (m // 4) * CH + ((m % 4) * 2 + k) * P
                            last = three(slot(m % 4, h * HALF, (h + 1) * HALF), w_hi[:, c:c + P], w_lo[:, c:c + P],
                                         tile(cv_r, gs + k, h * HALF, (h + 1) * HALF), tile(ga_r, gs + k, h * HALF, (h + 1) * HALF),
                                         k == 0, k == 1)
                    last.then_inc(w_used if m % 4 == 3 else dn_mm, 1)

            for s in range(2):
                up(s, s, N_FFN + 2 * s, None)

            def ffn(i):
                n = N_FFN + UPC + 12 * i
                for s in range(2):
                    up(4 * i + 2 + s, s, n + 2 * s, None if isinstance(i, int) else 16 * i - 3)
                down(2 * i, n + 4, 0)
                for s in range(2):
                    up(4 * i + 4 + s, s, n + 6 + 2 * s, 16 * i + 5)
                down(2 * i + 1, n + 10, 2)
            ffn(0)
            with pe.Fori(1, STEPS // 2) as i:
                ffn(i)
            q, n = STEPS - 1, NCHUNKS - 2
            pe.wait_ge(f_lo, 2 * q + 2)
            for m in range(KT):
                if m % 4 == 0:
                    pe.wait_ge(w_split, n + m // 4 + 1)
                pe.wait_ge(dn_ev, 8 * q + m - 3)
                for h in range(2):
                    for k in range(2):
                        c = (m // 4) * CH + ((m % 4) * 2 + k) * P
                        last = three(slot(m % 4, h * HALF, (h + 1) * HALF), w_hi[:, c:c + P], w_lo[:, c:c + P],
                                     tile(cv_r, k, h * HALF, (h + 1) * HALF), tile(ga_r, k, h * HALF, (h + 1) * HALF),
                                     k == 0, k == 1)
                last.then_inc(w_used if m % 4 == 3 else dn_mm, 1)
            pe.wait_ge(dn_ev, 8 * STEPS)
            for h in range(2):
                norm("nf", h)


def lay_out(np, x, w_in, b_in, conv_dw_w, conv_dw_b, conv_ln_g, conv_ln_b, conv_w_out, pool_w, pool_scale,
            mix_w_out, norm_mix, ffn_w_up, ffn_dw_w, ffn_dw_b, ffn_w_down, norm_ffn, norm_final):
    def block_tiles(w):
        k, n = w.shape
        return w.reshape(k // P, P, n // P, P).transpose(2, 1, 0, 3).reshape(n // P, P, k)

    a, b, c, ga, gb = (block_tiles(w_in[0][:, i * DM:(i + 1) * DM]) for i in range(5))
    chunks = list(c)
    for t in range(KT):
        chunks += [a[t], b[t], gb[t]]
    chunks += list(ga) + list(block_tiles(conv_w_out[0])) + list(block_tiles(mix_w_out[0]))
    up = block_tiles(ffn_w_up[0])
    dn = ffn_w_down[0].reshape(STEPS, CHUNK_PAIRS, P, 2, 4, P).transpose(0, 3, 2, 4, 1, 5).reshape(STEPS, 2, P, CH)

    def ups(q):
        return [t for p in range(CHUNK_PAIRS * q, CHUNK_PAIRS * (q + 1)) for t in (up[p], up[p + FT])]

    chunks += ups(0)
    for q in range(1, STEPS):
        chunks += ups(q) + list(dn[q - 1])
    chunks += list(dn[STEPS - 1])
    stream = np.ascontiguousarray(np.concatenate(chunks, axis=0))

    def per_channel(v):
        return v.reshape(-1, P).T

    edge = np.zeros((NG, WPAD), np.float32)
    for g, w in enumerate(WINDOWS):
        edge[g] = w / np.minimum(np.arange(1, WPAD + 1), w)
    params = np.ascontiguousarray(np.concatenate([
        per_channel(b_in[0]),
        conv_dw_w[0].reshape(TAPS, KT, P).transpose(2, 1, 0).reshape(P, KT * TAPS),
        per_channel(conv_dw_b[0]), per_channel(conv_ln_g[0]), per_channel(conv_ln_b[0]), per_channel(pool_scale[0]),
        per_channel(norm_mix[0]), per_channel(norm_ffn[0]), per_channel(norm_final),
        ffn_dw_w[0].reshape(3, 2 * FT, P).transpose(2, 1, 0).reshape(P, 2 * FT * 3),
        per_channel(ffn_dw_b[0]), np.broadcast_to(edge.reshape(1, -1), (P, NG * WPAD)),
    ], axis=1))
    pw = np.ascontiguousarray(pool_w[0].reshape(NG, 2, P, 2, P).transpose(2, 0, 1, 3, 4).reshape(P, 2 * CH))
    return {"xT": np.ascontiguousarray(x[0].T), "wstream": stream, "pool_w": pw, "params": params}


def kernel(**inputs):
    import numpy as np
    import concourse.bacc as bacc
    from concourse import mybir
    from concourse.bass_utils import run_bass_kernel_spmd

    arrays = lay_out(np, **{k: np.asarray(v) for k, v in inputs.items()})
    nc = bacc.Bacc("TRN2", target_bir_lowering=False, num_devices=1)
    args = [nc.dram_tensor(f"in_{n}", arrays[n].shape, mybir.dt.float32, kind="ExternalInput").ap()
            for n in ("xT", "wstream", "pool_w", "params")]
    out = nc.dram_tensor("outT", (DM, SEQ), mybir.dt.float32, kind="ExternalOutput").ap()
    build(nc, *args, out)
    r = run_bass_kernel_spmd(nc, [{f"in_{n}": a for n, a in arrays.items()}], core_ids=[0])
    return np.ascontiguousarray(r.results[0]["outT"].T)[None]
```

```python
EPS = 1e-6
P = 128
SEQ = 1024
HALF = SEQ // 2
DM = 1024
KT = DM // P
TAPS = 31
PAD = TAPS - 1
WINDOWS = (2, 4, 8, 16)
NG = len(WINDOWS)
WPAD = max(WINDOWS)
D_FF = 2816
FT = D_FF // P
CH = 8 * P
CHUNK_PAIRS = 2
STEPS = FT // CHUNK_PAIRS

_cols = {}
_n = 0
for _name, _w in (("b_in", 5 * KT), ("conv_w", KT * TAPS), ("conv_b", KT), ("ln_g", KT), ("ln_b", KT),
                  ("scale", KT), ("norm_mix", KT), ("norm_ffn", KT), ("norm_final", KT),
                  ("ffn_w", 2 * FT * 3), ("ffn_b", 2 * FT), ("edge", NG * WPAD)):
    _cols[_name] = _n
    _n += _w
NPAR = _n

FIRST_STEPS = 4
START = (("v", 0), ("g", 0), ("v", 1), ("g", 1), ("p", 0), ("p", 1), ("p", 2), ("p", 3), ("m", 0), ("p", 4), ("p", 5),
         ("m", 1), ("v", 2), ("g", 2), ("p", 6), ("p", 7), ("m", 2), ("v", 3), ("g", 3), ("m", 3), ("b", 0), ("b", 1))
STEP = (("v", 0), ("g", 0), ("a", -4), ("b", -2))
REST = (("a", 4), ("a", 5), ("b", 6), ("b", 7), ("a", 6), ("a", 7))

_part = {"v": 0, "g": 1, "p": 2, "a": 3, "b": 4}


def in_order():
    return list(START) + [(k, c + d) for c in range(FIRST_STEPS, KT) for k, d in STEP] + list(REST)


CHUNK, TURN = {}, {}
for _kind, _i in in_order():
    if _kind != "m":
        CHUNK[_kind, _i] = len(CHUNK)
    if _kind != "v":
        TURN[_kind, _i] = sum(2 if k == "m" else 1 for k, _ in TURN)
N_OUT = 5 * KT
N_MIX = N_OUT + KT
N_FFN = N_MIX + KT
UPC = 2 * CHUNK_PAIRS
DNC = 2
NCHUNKS = N_FFN + STEPS * (UPC + DNC)
STEP_TURNS = sum(k != "v" for k, _ in STEP)


def build(nc, xT, wstream, pool_w, params, outT):
    import concourse.bass as bass
    from concourse import mybir
    from contextlib import ExitStack

    f32, f32r = mybir.dt.float32, mybir.dt.float32r
    ACT = mybir.ActivationFunctionType
    ALU = mybir.AluOpType

    ctx = ExitStack()
    with ctx:
        def sb(name, cols, dt=f32):
            return ctx.enter_context(nc.sbuf_tensor(name, [P, cols], dt))

        def two_views(name_f32, name_f32r, cols):
            with nc.sbuf_tensor(name_f32, [P, cols], f32) as plain:
                pass
            return plain, sb(name_f32r, cols, f32r)

        def sem(name):
            return ctx.enter_context(nc.semaphore(name))

        def sems(*names):
            return [sem(n) for n in names]

        TS = KT * SEQ
        h_hi, h_lo = sb("h_hi", TS, f32r), sb("h_lo", TS, f32r)
        res = sb("res", TS)
        cv, cv_r = two_views("cv", "cv_r", TS)
        ga, ga_r = two_views("ga", "ga_r", TS)
        raw = sb("raw", 2 * CH)
        w_hi, w_lo = sb("w_hi", 2 * CH, f32r), sb("w_lo", 2 * CH, f32r)
        GLW = PAD + SEQ + 2
        tmp = sb("tmp", 2 * GLW + 2 * SEQ)
        par = sb("par", NPAR)
        ones = sb("ones", P)
        ident = sb("ident", P)
        small = sb("small", 64)
        ps = ctx.enter_context(nc.psum_tensor("ps", [P, 4 * SEQ], f32))

        def slot(n, a=0, b=SEQ):
            return ps[:, n * SEQ + a:n * SEQ + b]

        def bank(n, a=0, b=HALF):
            return ps[:, n * HALF + a:n * HALF + b]

        def tile(t, i, a=0, b=SEQ):
            return t[:, bass.ds(i * SEQ + a, b - a)]

        def span(h):
            return h * HALF, (h + 1) * HALF

        def par1(name, i):
            return par[:, bass.ds(i + _cols[name], 1)]

        csum = tmp[:, 2 * GLW:2 * GLW + SEQ]
        sgb = tmp[:, 2 * GLW + SEQ:2 * GLW + 2 * SEQ]

        def glu(c, a, n=SEQ):
            return tmp[:, bass.ds((c % 2) * GLW + a, n)]

        sq = [tmp[:, i * GLW:i * GLW + SEQ] for i in range(2)]
        diag = sgb
        acc_a = [tmp[:, i * SEQ:(i + 1) * SEQ] for i in range(2)]
        acc_b = [tmp[:, (2 + i) * SEQ:(3 + i) * SEQ] for i in range(2)]
        nt = [tmp[:, i * HALF:(i + 1) * HALF] for i in range(2)]
        n1_sq = [tmp[:, i * HALF:(i + 1) * HALF] for i in range(KT)]
        n1_nt = [cv[:, (8 + i) * HALF:(9 + i) * HALF] for i in range(4)]
        n1_diag = cv[:, 12 * HALF:13 * HALF]
        nf_sq = [tmp[:, i * HALF:(i + 1) * HALF] for i in range(2)]
        nf_sum = tmp[:, 2 * HALF:3 * HALF]
        nf_diag = tmp[:, 3 * HALF:4 * HALF]
        XW = WPAD + SEQ
        px = [cv[:, 4 * SEQ + i * XW:4 * SEQ + (i + 1) * XW] for i in range(2)]
        pst = [cv[:, 4 * SEQ + 2 * XW:4 * SEQ + 3 * XW], res[:, 6 * SEQ:6 * SEQ + XW]]
        pw_raw = res[:, 6 * SEQ:8 * SEQ]
        pp_hi = [ga_r[:, i * SEQ:(i + 1) * SEQ] for i in range(2)]
        pp_lo = [ga_r[:, (2 + i) * SEQ:(3 + i) * SEQ] for i in range(2)]
        pw_hi, pw_lo = ga_r[:, 4 * SEQ:6 * SEQ], ga_r[:, 6 * SEQ:8 * SEQ]

        par_loaded, pw_loaded, out_stored = sems("par_loaded", "pw_loaded", "out_stored")
        xre_loaded = sem("xre_loaded")
        x_loaded = [[sem(f"x_loaded{h}{q}") for q in range(2)] for h in range(2)]
        raw_loaded = [sem(f"raw_loaded{s}") for s in range(2)]
        split_go, w_hi_done, w_split, w_used = sems("split_go", "w_hi_done", "w_split", "w_used")
        consts, act_go = sems("consts", "act_go")
        s1_half, s1_out, pool_mm = sems("s1_half", "s1_out", "pool_mm")
        n1 = [{n: sem(f"n1_{h}_{n}") for n in ("sq_a", "sq_v", "ss", "std", "rinv", "diag", "bc", "val", "hi", "lo")} for h in range(2)]
        pads, sums, pw_hi_done, pw_lo_done, p_mean, p_hi, p_lo = sems(
            "pads", "sums", "pw_hi_done", "pw_lo_done", "p_mean", "p_hi", "p_lo")
        glu_done, conv_init, conv_tap, acc_free, cv_done, cv_merged, cs_done, gb_done = sems(
            "glu_done", "conv_init", "conv_tap", "acc_free", "cv_done", "cv_merged", "cs_done", "gb_done")
        ln = {n: sem("ln_" + n) for n in ("mean", "d", "sq", "sum", "ss", "std", "rinv", "diag", "bc", "n", "z")}
        z_hi, z_lo = sems("z_hi", "z_lo")
        co_a, co_m, co_hi, co_lo = sems("co_a", "co_m", "co_hi", "co_lo")
        x1_done = sem("x1_done")
        n2 = {n: sem("n2_" + n) for n in ("zero", "sq", "sum", "ss", "std", "rinv", "diag", "bc", "val", "hi", "lo")}
        f_acca, f_accb, f_ca1, f_ca, f_cb1, f_cb, f_gelu, f_g, f_hi, f_lo, dn_mm, dn_ev = sems(
            "f_acca", "f_accb", "f_ca1", "f_ca", "f_cb1", "f_cb", "f_gelu", "f_g", "f_hi", "f_lo", "dn_mm", "dn_ev")
        x2_mm, x2_done = sems("x2_mm", "x2_done")
        nf = [{n: sem(f"nf_{h}_{n}") for n in ("zero", "sq", "sum", "ss", "std", "rinv", "diag", "bc", "out")} for h in range(2)]

        block = ctx.enter_context(nc.Block())

        def wait(eng, s, v):
            if not (isinstance(v, int) and v <= 0):
                eng.wait_ge(s, v)

        def out_of(turn):
            return 2 * turn + 2

        @block.sync
        def _(sp):
            x_s, x_d = res[:, :].rearrange("p (k n) -> p k n", k=KT), xT.rearrange("(k p) n -> p k n", p=P)
            for h in range(2):
                for q in range(2):
                    k, (a, b) = slice(4 * q, 4 * q + 4), span(h)
                    sp.dma_start(x_s[:, k, a:b], x_d[:, k, a:b]).then_inc(x_loaded[h][q], 16)
                if h == 0:
                    sp.dma_start(par[:, :], params).then_inc(par_loaded, 16)
                    for s in range(2):
                        sp.dma_start(raw[:, s * CH:(s + 1) * CH], wstream[s * P:(s + 1) * P, :]).then_inc(raw_loaded[s], 16)
            with sp.Fori(1, NCHUNKS // 2) as i:
                for s in range(2):
                    sp.wait_ge(w_split, 2 * i + s - 1)
                    sp.dma_start(raw[:, s * CH:(s + 1) * CH],
                                 wstream[bass.ds((2 * i + s) * P, P), :]).then_inc(raw_loaded[s], 16)
            o_d = outT.rearrange("(k p) n -> p k n", p=P)
            for h in range(2):
                for q in range(4):
                    k, (a, b) = slice(2 * q, 2 * q + 2), span(h)
                    sp.wait_ge(nf[h]["out"], 2 * (q + 1))
                    sp.dma_start(o_d[:, k, a:b], x_s[:, k, a:b]).then_inc(out_stored, 16)
            sp.wait_ge(out_stored, 128)

        @block.gpsimd
        def _(pool):
            pool.memset(ones[:, :], 1.0).then_inc(consts, 1)
            pool.memset(small[:, 60:61], EPS).then_inc(consts, 1)
            pool.memset(ident[:, :], 0.0).then_inc(consts, 1)
            pool.wait_ge(consts, 3)
            pool.affine_select(out=ident[:, :], in_=ident[:, :], compare_op=ALU.not_equal, fill=1.0,
                               base=0, pattern=[[-1, P]], channel_multiplier=1).then_inc(consts, 1)

            def split(n, s, i):
                pool.wait_ge(raw_loaded[s], 16 * (i + 1))
                wait(pool, w_used, n - 1)
                pool.sem_inc(split_go, 1)
                r, hi, lo = (t[:, s * CH:(s + 1) * CH] for t in (raw, w_hi, w_lo))
                pool.tensor_scalar(hi, r, 1.0, 0.0, ALU.mult, ALU.add).then_inc(w_hi_done, 1)
                pool.wait_ge(w_hi_done, n + 1)
                pool.tensor_tensor(lo, r, hi.bitcast(f32), ALU.subtract).then_inc(w_split, 1)

            for s in range(2):
                split(s, s, 0)
            pool.wait_ge(n1[0]["lo"], KT)
            pool.wait_ge(n1[1]["lo"], KT)
            pool.dma_start(pw_raw, pool_w).then_inc(pw_loaded, 16)
            with pool.Fori(1, NCHUNKS // 2) as i:
                for s in range(2):
                    split(2 * i + s, s, i)
            for h in range(2):
                for m in range(KT):
                    pool.wait_ge(nf[h]["sq"], m + 1)
                    if m:
                        pool.wait_ge(nf[h]["sum"], m)
                    else:
                        pool.wait_ge(nf[h]["zero"], 1)
                    pool.tensor_tensor(nf_sum, nf_sum, nf_sq[m % 2], ALU.add).then_inc(nf[h]["sum"], 1)

        @block.scalar
        def _(act):
            eps = small[:, 60:61]

            def square1(h, k):
                act.wait_ge(x_loaded[h][k // 4], 16)
                if h:
                    act.wait_ge(n1[0]["ss"], 1)
                act.activation(n1_sq[k], tile(res, k, *span(h)), ACT.Square).then_inc(n1[h]["sq_a"], 1)

            def deviation1(h):
                act.wait_ge(n1[h]["ss"], 1)
                act.activation(small[:, 8 * h:8 * h + 4], bank(4 + 2 * h, 0, 4), ACT.Sqrt, bias=eps, scale=1.0 / DM).then_inc(n1[h]["std"], 1)

            def high1(h, k):
                act.wait_ge(n1[h]["val"], k + 1)
                act.activation(tile(h_hi, k, *span(h)), n1_nt[k % 4], ACT.Copy).then_inc(n1[h]["hi"], 1)

            act.wait_ge(consts, 4)
            for k in range(0, KT, 2):
                square1(0, k)
            deviation1(0)
            for k in range(KT):
                high1(0, k)
                square1(1, k)
            deviation1(1)
            for k in range(KT):
                high1(1, k)

            def hold(i):
                if not isinstance(i, int):
                    act.sem_inc(act_go, 1)

            def read_out(turn, second, second_val, out_ap, func, **kw):
                for h in range(2):
                    act.wait_ge(*((s1_half, turn + 1) if h == 0 else (second, second_val)))
                    hold(turn)
                    act.activation(out_ap[:, h * HALF:(h + 1) * HALF], slot(1, *span(h)), func, **kw).then_inc(s1_out, 1)

            def gate(c, turn, n):
                read_out(turn, w_used, n + 1, tile(cv, c), ACT.Sigmoid, bias=par1("b_in", KT + c))

            def gate_a(c, turn, n):
                read_out(turn, w_used, n + 1, tile(ga, c), ACT.Sigmoid, bias=par1("b_in", 3 * KT + c))

            def gate_b(c, turn, n):
                wait(act, gb_done, c)
                read_out(turn, w_used, n + 1, sgb, ACT.Sigmoid, bias=par1("b_in", 4 * KT + c))

            def pool_in(t, turn, n):
                wait(act, p_lo, 2 * (t // 2))
                read_out(turn, w_used, n + 1, px[t % 2][:, WPAD:], ACT.Identity, bias=par1("b_in", 2 * KT + t))

            def pool_hi(g):
                for j in range(2):
                    act.wait_ge(p_mean, 2 * g + j + 1)
                    wait(act, pool_mm, 2 * g)
                    act.activation(pp_hi[j], px[j][:, WPAD:], ACT.Copy).then_inc(p_hi, 1)

            def pool_out(g, turn):
                for m in range(2):
                    read_out(turn + m, pool_mm, 2 * g + m + 1, tile(res, 2 * g + m), ACT.Copy, scale=par1("scale", 2 * g + m))

            def init_conv(c):
                act.wait_ge(glu_done, c + 1)
                for j in range(2):
                    wait(act, acc_free, 2 * c + j - 1) if isinstance(c, int) else act.wait_ge(acc_free, 2 * c + j - 1)
                    hold(c)
                    if j == 0:
                        act.activation(slot(2), glu(c, PAD), ACT.Identity, bias=par1("conv_b", c),
                                       scale=par1("conv_w", c * TAPS + PAD)).then_inc(conv_init, 1)
                    else:
                        act.activation(slot(3), glu(c, PAD - 1), ACT.Copy, scale=par1("conv_w", c * TAPS + PAD - 1)).then_inc(conv_init, 1)

            handlers = {"g": gate, "a": gate_a, "b": gate_b, "p": pool_in}
            for kind, i in START:
                if kind == "m":
                    pool_out(i, TURN[kind, i])
                elif kind != "v":
                    handlers[kind](i, TURN[kind, i], CHUNK[kind, i])
                if (kind, i) == ("g", 0):
                    init_conv(0)
                if (kind, i) == ("g", 1):
                    act.wait_ge(pw_loaded, 16)
                    act.activation(pw_hi, pw_raw, ACT.Copy).then_inc(pw_hi_done, 1)
                if kind == "p" and i == 1:
                    init_conv(1)
                    pool_hi(0)
                if (kind, i) == ("m", 0):
                    pool_hi(1)
                if (kind, i) == ("m", 1):
                    pool_hi(2)
                if kind == "g" and i >= 2:
                    init_conv(i)
                if (kind, i) == ("m", 2):
                    pool_hi(3)
            act.wait_ge(pool_mm, 2 * NG)
            with act.Fori(FIRST_STEPS, KT) as c:
                for j, (kind, d) in enumerate(STEP):
                    if kind != "v":
                        turn = c * STEP_TURNS + (TURN[kind, FIRST_STEPS + d] - STEP_TURNS * FIRST_STEPS)
                        handlers[kind](c + d, turn, c * len(STEP) + (CHUNK["v", FIRST_STEPS] + j - len(STEP) * FIRST_STEPS))
                    if kind == "a":
                        init_conv(c)

            def rest(kind, i):
                handlers[kind](i, TURN[kind, i], CHUNK[kind, i])

            rest("a", 4)
            rest("a", 5)
            for c in range(KT):
                act.wait_ge(ln["d"], c + 1)
                if c >= 2:
                    act.wait_ge(ln["sum"], c - 1)
                act.activation(sq[c % 2], tile(cv, c), ACT.Square).then_inc(ln["sq"], 1)
                if c == 3:
                    rest("b", 6)
            rest("b", 7)
            act.wait_ge(ln["ss"], 1)
            act.activation(small[:, 16:16 + KT], slot(3, 0, KT), ACT.Sqrt, bias=eps, scale=1.0 / DM).then_inc(ln["std"], 1)
            rest("a", 6)
            silu = dict(func=ACT.Silu)
            for c in range(KT):
                act.wait_ge(ln["n"], c + 1)
                act.activation(tile(cv, c), tile(cv, c), bias=par1("ln_b", c), scale=par1("ln_g", c), **silu).then_inc(ln["z"], 1)
            rest("a", 7)
            for h in range(2):
                for c in range(KT):
                    act.wait_ge(ln["z"], c + 1)
                    act.activation(tile(h_hi, c, *span(h)), tile(cv, c, *span(h)), ACT.Copy).then_inc(z_hi, 1)

            act.wait_ge(z_lo, 2 * KT)
            xr = xT.rearrange("(k p) n -> p k n", p=P)
            with act.Fori(0, KT // 2) as i:
                for j in range(2):
                    act.wait_ge(co_m, 2 * i + j + 1)
                    act.activation(tile(cv_r, 2 * i + j), tile(res, 2 * i + j), ACT.Copy).then_inc(co_hi, 1)
                act.wait_ge(co_lo, 2 * i + 2)
                act.dma_start(res[:, bass.ds(2 * i * SEQ, 2 * SEQ)].rearrange("p (k n) -> p k n", k=2),
                              xr[:, bass.ds(2 * i, 2), :]).then_inc(xre_loaded, 16)

            for k in range(KT):
                act.wait_ge(x1_done, k + 1)
                if k >= 2:
                    act.wait_ge(n2["sum"], k - 1)
                act.activation(sq[k % 2], tile(res, k), ACT.Square).then_inc(n2["sq"], 1)
            act.wait_ge(n2["ss"], 1)
            act.activation(small[:, 32:32 + KT], slot(3, 0, KT), ACT.Sqrt, bias=eps, scale=1.0 / DM).then_inc(n2["std"], 1)
            for h in range(2):
                for k in range(KT):
                    act.wait_ge(n2["val"], h * KT + k + 1)
                    act.activation(tile(h_hi, k, *span(h)), nt[k % 2], ACT.Copy).then_inc(n2["hi"], 1)

            def up(p, s, gs, n, dn_need):
                act.wait_ge(w_used, n + 1)
                wait(act, f_g, p - 1)
                act.activation(acc_a[s], slot(2 * s), ACT.Identity, bias=par1("ffn_b", p), scale=par1("ffn_w", p * 3 + 2)).then_inc(f_acca, 1)
                act.wait_ge(f_ca, p + 1)
                act.activation(acc_a[s], acc_a[s], ACT.Gelu_apprx_tanh).then_inc(f_gelu, 1)
                act.wait_ge(w_used, n + 2)
                wait(act, f_lo, p - 1)
                act.activation(acc_b[s], slot(2 * s + 1), ACT.Identity, bias=par1("ffn_b", p + FT), scale=par1("ffn_w", (p + FT) * 3 + 2)).then_inc(f_accb, 1)
                act.wait_ge(f_g, p + 1)
                if dn_need is not None:
                    act.wait_ge(w_used, dn_need)
                act.activation(tile(cv_r, gs), acc_b[s], ACT.Copy).then_inc(f_hi, 1)

            act.wait_ge(n2["lo"], 2 * KT)
            up(0, 0, 0, N_FFN, None)
            up(1, 1, 1, N_FFN + 2, None)

            def ffn(i):
                n = N_FFN + UPC + 12 * i
                for s in range(2):
                    up(4 * i + 2 + s, s, 2 + s, n + 2 * s, None if isinstance(i, int) else n)
                for s in range(2):
                    up(4 * i + 4 + s, s, s, n + 6 + 2 * s, n + 6)
            ffn(0)
            with act.Fori(1, STEPS // 2) as i:
                ffn(i)

            for h in range(2):
                z = nf[h]
                act.wait_ge(z["zero"], 1)
                for m in range(KT):
                    act.wait_ge(x2_done, h * KT + m + 1)
                    if m >= 2:
                        act.wait_ge(z["sum"], m - 1)
                    act.activation(nf_sq[m % 2], tile(res, m, *span(h)), ACT.Square).then_inc(z["sq"], 1)
                act.wait_ge(z["ss"], 1)
                act.activation(small[:, 40 + 8 * h:44 + 8 * h], bank(6, 0, 4), ACT.Sqrt, bias=eps, scale=1.0 / DM).then_inc(z["std"], 1)

        @block.vector
        def _(dve):
            def invert(z, std, n, dst, fresh=None):
                dve.wait_ge(z["std"], 1)
                dve.reciprocal(small[:, std + n:std + 2 * n], small[:, std:std + n]).then_inc(z["rinv"], 1)
                dve.wait_ge(z["rinv"], 1)
                if fresh:
                    dve.wait_ge(*fresh)
                for j in range(n):
                    dve.tensor_scalar(dst[:, j * P:(j + 1) * P], ident[:, :], small[:, std + n + j:std + n + j + 1], None,
                                      ALU.mult).then_inc(z["diag"], 1)

            def normed(z, h, gain, src_bc, bufs, base):
                def low(k):
                    dve.wait_ge(z["hi"], base + k + 1)
                    dve.tensor_tensor(tile(h_lo, k, *span(h)), bufs[k % len(bufs)], tile(h_hi, k, *span(h)).bitcast(f32),
                                      ALU.subtract).then_inc(z["lo"], 1)
                for k in range(KT):
                    wait(dve, z["lo"], base + k - len(bufs) + 1)
                    dve.scalar_tensor_tensor(out=bufs[k % len(bufs)], in0=tile(res, k, *span(h)), scalar=par1(gain, k),
                                             in1=src_bc, op0=ALU.mult, op1=ALU.mult).then_inc(z["val"], 1)
                    if k:
                        low(k - 1)
                low(KT - 1)

            dve.wait_ge(consts, 4)
            for k in range(1, KT, 2):
                dve.wait_ge(x_loaded[0][k // 4], 16)
                dve.tensor_tensor(n1_sq[k], tile(res, k, *span(0)), tile(res, k, *span(0)), ALU.mult).then_inc(n1[0]["sq_v"], 1)
            dve.wait_ge(par_loaded, 16)
            for h in range(2):
                invert(n1[h], 8 * h, 4, n1_diag, (n1[0]["bc"], 1) if h else None)
                dve.wait_ge(n1[h]["bc"], 1)
                if h:
                    dve.wait_ge(n1[0]["lo"], KT)
                normed(n1[h], h, "norm_mix", bank(5 + 2 * h), n1_nt, 0)
            dve.wait_ge(n1[1]["lo"], KT)
            for c in range(2):
                dve.memset(glu(c, 0, PAD), 0.0).then_inc(pads, 1)
            dve.memset(csum, 0.0).then_inc(pads, 1)
            for t in px + pst[:1]:
                dve.memset(t[:, 0:WPAD], 0.0).then_inc(pads, 1)
            dve.wait_ge(pads, 6)

            def make_glu(c, turn):
                dve.wait_ge(s1_out, out_of(turn))
                wait(dve, cs_done, c - 1)
                dve.scalar_tensor_tensor(out=glu(c, PAD), in0=slot(0), scalar=par1("b_in", c), in1=tile(cv, c),
                                         op0=ALU.add, op1=ALU.mult).then_inc(glu_done, 1)

            def times_gate_b(c, turn):
                dve.wait_ge(s1_out, out_of(turn))
                dve.tensor_tensor(tile(res, c), sgb, tile(res, c), ALU.mult).then_inc(gb_done, 1)

            def conv(c, between):
                base = c * (TAPS - 3)
                dve.wait_ge(conv_init, 2 * c + 1)
                for t in range(TAPS - 2):
                    if t in between:
                        between[t]()
                    if t == 1:
                        dve.wait_ge(conv_init, 2 * c + 2)
                    if t >= 2:
                        dve.wait_ge(conv_tap, base + t - 1)
                    acc = slot(2 + t % 2)
                    dst = acc if t < TAPS - 3 else tile(cv, c)
                    dve.scalar_tensor_tensor(out=dst, in0=glu(c, t), scalar=par1("conv_w", c * TAPS + t), in1=acc,
                                             op0=ALU.mult, op1=ALU.add).then_inc(conv_tap if t < TAPS - 3 else acc_free, 1)
                dve.wait_ge(acc_free, 2 * c + 1)
                dve.wait_ge(conv_tap, base + TAPS - 3)
                dve.tensor_tensor(tile(cv, c), slot(3), tile(cv, c), ALU.add).then_inc(acc_free, 1)
                dve.wait_ge(acc_free, 2 * c + 2)
                dve.tensor_tensor(csum, csum, tile(cv, c), ALU.add).then_inc(cs_done, 1)

            n_sums = [0]

            def added(ins):
                n_sums[0] += 1
                ins.then_inc(sums, 1)
                dve.wait_ge(sums, n_sums[0])

            def pool_mean(g):
                w = WINDOWS[g]
                for j in range(2):
                    dve.wait_ge(s1_out, out_of(TURN["p", 2 * g + j]))
                    src, d, n = px[j], 1, 0
                    while d < w:
                        added(dve.tensor_tensor(pst[n][:, WPAD:], src[:, WPAD:], src[:, WPAD - d:WPAD - d + SEQ], ALU.add))
                        src, d, n = pst[n], 2 * d, 1 - n
                    e = _cols["edge"] + g * WPAD
                    added(dve.tensor_tensor(src[:, WPAD:2 * WPAD], src[:, WPAD:2 * WPAD], par[:, e:e + WPAD], ALU.mult))
                    dve.scalar_tensor_tensor(out=px[j][:, WPAD:], in0=src[:, WPAD:], scalar=1.0 / w, in1=px[j][:, WPAD:],
                                             op0=ALU.mult, op1=ALU.subtract).then_inc(p_mean, 1)
                    dve.wait_ge(p_mean, 2 * g + j + 1)

            def pool_low(g):
                for j in range(2):
                    dve.wait_ge(p_hi, 2 * g + j + 1)
                    wait(dve, pool_mm, 2 * g)
                    dve.tensor_tensor(pp_lo[j], px[j][:, WPAD:], pp_hi[j].bitcast(f32), ALU.subtract).then_inc(p_lo, 1)

            def split_pool_w():
                dve.wait_ge(pw_hi_done, 1)
                dve.tensor_tensor(pw_lo, pw_raw, pw_hi.bitcast(f32), ALU.subtract).then_inc(pw_lo_done, 1)
                dve.wait_ge(pw_lo_done, 1)
                dve.memset(pst[1][:, 0:WPAD], 0.0).then_inc(pads, 1)
                dve.wait_ge(pads, 7)

            make_glu(0, TURN["g", 0])
            conv(0, {22: lambda: make_glu(1, TURN["g", 1]), 27: split_pool_w})
            pool_mean(0)
            conv(1, {0: lambda: pool_low(0), 11: lambda: pool_mean(1), 14: lambda: pool_low(1),
                     20: lambda: pool_mean(2), 23: lambda: pool_low(2), 26: lambda: make_glu(2, TURN["g", 2])})
            conv(2, {16: lambda: pool_mean(3), 19: lambda: pool_low(3), 26: lambda: make_glu(3, TURN["g", 3])})
            conv(3, {10: lambda: times_gate_b(0, TURN["b", 0]), 20: lambda: times_gate_b(1, TURN["b", 1]),
                     27: lambda: make_glu(4, TURN["g", 4])})

            def step_turn(kind, d, c):
                return c * STEP_TURNS + (TURN[kind, FIRST_STEPS + d] - STEP_TURNS * FIRST_STEPS)

            with dve.Fori(FIRST_STEPS, KT - 1) as c:
                conv(c, {12: lambda: times_gate_b(c - 2, step_turn("b", -2, c)),
                         24: lambda: make_glu(c + 1, step_turn("g", 0, c + 1))})
            conv(KT - 1, {12: lambda: times_gate_b(KT - 3, TURN["b", KT - 3])})

            dve.wait_ge(ln["mean"], 1)

            def centre(c):
                dve.scalar_tensor_tensor(out=tile(cv, c), in0=slot(2), scalar=-1.0 / DM, in1=tile(cv, c),
                                         op0=ALU.mult, op1=ALU.add).then_inc(ln["d"], 1)

            def add_square(z, k, first=False):
                dve.wait_ge(z["sq"], k + 1)
                wait(dve, z["sum"], k)
                if k == 0:
                    dve.tensor_copy(csum, sq[0]).then_inc(z["sum"], 1)
                else:
                    dve.tensor_tensor(csum, csum, sq[k % 2], ALU.add).then_inc(z["sum"], 1)

            for c in range(KT):
                centre(c)
                if c:
                    add_square(ln, c - 1)
                if c == 5:
                    times_gate_b(6, TURN["b", 6])
            add_square(ln, KT - 1)
            times_gate_b(7, TURN["b", 7])
            invert(ln, 16, KT, diag, (gb_done, KT))
            dve.wait_ge(ln["bc"], 1)
            for c in range(KT):
                dve.tensor_tensor(tile(cv, c), slot(2), tile(cv, c), ALU.mult).then_inc(ln["n"], 1)
            for h in range(2):
                for c in range(KT):
                    dve.wait_ge(z_hi, h * KT + c + 1)
                    dve.tensor_tensor(tile(h_lo, c, *span(h)), tile(cv, c, *span(h)), tile(h_hi, c, *span(h)).bitcast(f32),
                                      ALU.subtract).then_inc(z_lo, 1)

            dve.wait_ge(s1_out, out_of(TURN["a", KT - 1]))
            with dve.Fori(0, KT // 2) as i:
                for j in range(2):
                    m = 2 * i + j
                    dve.wait_ge(w_used, N_OUT + m + 1)
                    dve.tensor_tensor(tile(ga, m), slot(j), tile(ga, m), ALU.mult).then_inc(co_a, 1)
                    dve.wait_ge(co_a, m + 1)
                    dve.tensor_tensor(tile(res, m), tile(ga, m), tile(res, m), ALU.add).then_inc(co_m, 1)
                    dve.wait_ge(co_hi, m + 1)
                    dve.tensor_tensor(tile(ga_r, m), tile(res, m), tile(cv_r, m).bitcast(f32), ALU.subtract).then_inc(co_lo, 1)

            dve.wait_ge(xre_loaded, 16 * (KT // 2))
            for m in range(KT):
                dve.wait_ge(w_used, N_MIX + m + 1)
                dve.tensor_tensor(tile(res, m), slot(m % 2), tile(res, m), ALU.add).then_inc(x1_done, 1)
                if m:
                    add_square(n2, m - 1)
            add_square(n2, KT - 1)
            invert(n2, 32, KT, diag)
            for h in range(2):
                dve.wait_ge(n2["bc"], h + 1)
                normed(n2, h, "norm_ffn", slot(2, *span(h)), nt, h * KT)

            def up(p, s, gs):
                for f, acc, started, first_tap, done, n in ((p, acc_a[s], f_acca, f_ca1, f_ca, 2 * s),
                                                            (p + FT, acc_b[s], f_accb, f_cb1, f_cb, 2 * s + 1)):
                    dve.wait_ge(started, p + 1)
                    for d, s_done in ((1, first_tap), (2, done)):
                        dve.scalar_tensor_tensor(out=acc[:, d:], in0=slot(n, 0, SEQ - d), scalar=par1("ffn_w", f * 3 + 2 - d),
                                                 in1=acc[:, d:], op0=ALU.mult, op1=ALU.add).then_inc(s_done, 1)
                        if d == 1:
                            dve.wait_ge(s_done, p + 1)
                dve.wait_ge(f_gelu, p + 1)
                dve.wait_ge(f_cb, p + 1)
                dve.tensor_tensor(acc_b[s], acc_a[s], acc_b[s], ALU.mult).then_inc(f_g, 1)
                dve.wait_ge(f_hi, p + 1)
                dve.tensor_tensor(tile(ga_r, gs), acc_b[s], tile(cv_r, gs).bitcast(f32), ALU.subtract).then_inc(f_lo, 1)

            def down(q, n):
                for m in range(KT):
                    if m % 4 == 3:
                        dve.wait_ge(w_used, n + m // 4 + 1)
                    else:
                        dve.wait_ge(dn_mm, 6 * q + m - m // 4 + 1)
                    wait(dve, dn_ev, 8 * q + m)
                    dve.tensor_tensor(tile(res, m), slot(m % 4), tile(res, m), ALU.add).then_inc(dn_ev, 1)

            dve.wait_ge(n2["lo"], 2 * KT)
            for s in range(2):
                up(s, s, s)

            def ffn(i):
                n = N_FFN + UPC + 12 * i
                for s in range(2):
                    up(4 * i + 2 + s, s, 2 + s)
                down(2 * i, n + 4)
                for s in range(2):
                    up(4 * i + 4 + s, s, s)
                down(2 * i + 1, n + 10)
            ffn(0)
            with dve.Fori(1, STEPS // 2) as i:
                ffn(i)

            dve.wait_ge(dn_ev, 8 * (STEPS - 1))

            def last_add(h, m):
                dve.wait_ge(x2_mm, h * KT + m + 1)
                t = tile(res, m, *span(h))
                dve.tensor_tensor(t, bank((h * KT + m) % 6), t, ALU.add).then_inc(x2_done, 1)

            def final(h, k):
                if k == 0:
                    dve.wait_ge(nf[h]["bc"], 1)
                t = tile(res, k, *span(h))
                dve.scalar_tensor_tensor(out=t, in0=t, scalar=par1("norm_final", k), in1=bank(7),
                                         op0=ALU.mult, op1=ALU.mult).then_inc(nf[h]["out"], 1)

            dve.memset(nf_sum, 0.0).then_inc(nf[0]["zero"], 1)
            for m in range(KT):
                last_add(0, m)
            for m in range(3):
                last_add(1, m)
            invert(nf[0], 40, 4, nf_diag)
            dve.wait_ge(nf[0]["ss"], 1)
            dve.memset(nf_sum, 0.0).then_inc(nf[1]["zero"], 1)
            for m in range(3, KT):
                last_add(1, m)
                final(0, m - 3)
            for k in range(KT - 3, KT):
                final(0, k)
            invert(nf[1], 48, 4, nf_diag, (nf[0]["bc"], 1))
            for k in range(KT):
                final(1, k)

        @block.tensor
        def _(pe):
            def three(out, a_hi, a_lo, b_hi, b_lo, start, stop):
                nc.tensor.matmul(out, a_hi, b_lo, start=start, stop=False)
                nc.tensor.matmul(out, a_lo, b_hi, start=False, stop=False)
                return nc.tensor.matmul(out, a_hi, b_hi, start=False, stop=stop)

            def half_tile(s, out, h, mov_hi, mov_lo, ready=None):
                for k in range(KT):
                    if ready:
                        pe.wait_ge(*ready(h, k))
                    c = s * CH + k * P
                    last = three(out, w_hi[:, c:c + P], w_lo[:, c:c + P],
                                 tile(mov_hi, k, *span(h)), tile(mov_lo, k, *span(h)), k == 0, k == KT - 1)
                return last

            def project(n, s, dst, mov_hi, mov_lo, ready=None):
                pe.wait_ge(w_split, n + 1)
                for h in range(2):
                    last = half_tile(s, slot(dst, *span(h)), h, mov_hi, mov_lo, ready)
                last.then_inc(w_used, 1)

            def first_pair(n, dst, ready, half_sem=None):
                for h in range(2):
                    for j in range(2):
                        if h == 0:
                            pe.wait_ge(w_split, n + j + 1)
                        last = half_tile((n + j) % 2, slot(dst + j, *span(h)), h, h_hi, h_lo, ready if j == 0 else None)
                        if h:
                            last.then_inc(w_used, 1)
                        elif j and half_sem:
                            last.then_inc(half_sem, 1)

            def sum_positions(dst, src, n, done):
                for j in range(n):
                    last = nc.tensor.matmul(dst[:, j:j + 1], src[:, j * P:(j + 1) * P], ones[:, 0:1],
                                            start=True, stop=True)
                last.then_inc(done, 1)

            pe.wait_ge(consts, 4)
            for h in range(2):
                z = n1[h]
                for k in range(KT):
                    if h:
                        pe.wait_ge(z["sq_a"], k + 1)
                    else:
                        pe.wait_ge(z["sq_v"] if k % 2 else z["sq_a"], k // 2 + 1)
                    for j in range(4):
                        last = nc.tensor.matmul(bank(4 + 2 * h, j, j + 1), n1_sq[k][:, j * P:(j + 1) * P], ones[:, 0:1],
                                                start=(k == 0 and j == 0), stop=(k == KT - 1), skip_group_check=True)
                last.then_inc(z["ss"], 1)
                if h == 0:
                    pe.wait_ge(z["diag"], 4)
                    nc.tensor.matmul(bank(5), ones[:, :], n1_diag, start=True, stop=True).then_inc(z["bc"], 1)
            z = n1[1]
            pe.wait_ge(z["diag"], 4)
            nc.tensor.matmul(bank(7), ones[:, :], n1_diag, start=True, stop=True).then_inc(z["bc"], 1)

            def through_slot1(kind_n, s, turn):
                pe.wait_ge(w_split, kind_n + 1)
                for h in range(2):
                    wait(pe, s1_out, 2 * turn + h - 1)
                    last = half_tile(s, slot(1, *span(h)), h, h_hi, h_lo)
                    last.then_inc(w_used if h else s1_half, 1)

            def value(c, n, s):
                wait(pe, glu_done, c)
                project(n, s, 0, h_hi, h_lo)

            def pool_map(g, turn):
                pe.wait_ge(pw_lo_done, 1)
                pe.wait_ge(p_lo, 2 * (g + 1))
                for m in range(2):
                    for h in range(2):
                        pe.wait_ge(s1_out, 2 * (turn + m) + h - 1)
                        for k in range(2):
                            c = g * 4 * P + (2 * k + m) * P
                            last = three(slot(1, *span(h)), pw_hi[:, c:c + P], pw_lo[:, c:c + P],
                                         pp_hi[k][:, h * HALF:(h + 1) * HALF], pp_lo[k][:, h * HALF:(h + 1) * HALF],
                                         k == 0, k == 1)
                        last.then_inc(pool_mm if h else s1_half, 1)

            first_pair(0, 0, lambda h, k: (n1[h]["lo"], k + 1), s1_half)
            for kind, i in START[2:]:
                if kind == "m":
                    pool_map(i, TURN[kind, i])
                elif kind == "v":
                    value(i, CHUNK[kind, i], CHUNK[kind, i] % 2)
                else:
                    through_slot1(CHUNK[kind, i], CHUNK[kind, i] % 2, TURN[kind, i])
            with pe.Fori(FIRST_STEPS, KT) as c:
                for j, (kind, d) in enumerate(STEP):
                    n = c * len(STEP) + (CHUNK["v", FIRST_STEPS] + j - len(STEP) * FIRST_STEPS)
                    if kind == "v":
                        value(c, n, j % 2)
                    else:
                        through_slot1(n, j % 2, c * STEP_TURNS + (TURN[kind, FIRST_STEPS + d] - STEP_TURNS * FIRST_STEPS))

            def rest(kind, i):
                through_slot1(CHUNK[kind, i], CHUNK[kind, i] % 2, TURN[kind, i])

            rest("a", 4)
            rest("a", 5)
            pe.wait_ge(cs_done, KT)
            for h in range(2):
                last = nc.tensor.matmul(slot(2, *span(h)), ones[:, :], csum[:, h * HALF:(h + 1) * HALF], start=True, stop=True)
            last.then_inc(ln["mean"], 1)
            rest("b", 6)
            rest("b", 7)
            pe.wait_ge(ln["sum"], KT)
            sum_positions(slot(3, 0, KT), csum, KT, ln["ss"])
            rest("a", 6)
            pe.wait_ge(ln["diag"], KT)
            for h in range(2):
                last = nc.tensor.matmul(slot(2, *span(h)), ones[:, :], diag[:, h * HALF:(h + 1) * HALF], start=True, stop=True)
            last.then_inc(ln["bc"], 1)
            rest("a", 7)

            def pairs(first_n, read_out, mov_hi, mov_lo, ready):
                def two(i):
                    for j in range(2):
                        wait(pe, read_out, 2 * i + j - 1)
                        project(first_n + 2 * i + j, j, j, mov_hi, mov_lo, ready if isinstance(i, int) and j == 0 else None)
                two(0)
                with pe.Fori(1, KT // 2) as i:
                    two(i)

            pe.wait_ge(glu_done, KT)
            pe.wait_ge(s1_out, out_of(TURN["a", KT - 1]))
            pairs(N_OUT, co_a, h_hi, h_lo, lambda h, k: (z_lo, h * KT + k + 1))
            pe.wait_ge(co_a, KT)
            pairs(N_MIX, x1_done, cv_r, ga_r, lambda h, k: (co_lo, k + 1))
            pe.wait_ge(n2["sum"], KT)
            sum_positions(slot(3, 0, KT), csum, KT, n2["ss"])
            for h in range(2):
                pe.wait_ge(n2["diag"], 4 * (h + 1))
                nc.tensor.matmul(slot(2, *span(h)), ones[:, :], diag[:, h * HALF:(h + 1) * HALF], start=True, stop=True).then_inc(n2["bc"], 1)

            def up(p, s, n, dn):
                wait(pe, f_cb, p - 1)
                for j in range(2):
                    if dn is not None:
                        pe.wait_ge(dn_ev, dn + 2 * s + j)
                    project(n + j, j, 2 * s + j, h_hi, h_lo)

            def down(q, n, gs):
                pe.wait_ge(f_lo, 2 * q + 2)
                for m in range(KT):
                    if m % 4 == 0:
                        pe.wait_ge(w_split, n + m // 4 + 1)
                    if m < 4:
                        pe.wait_ge(f_cb, 2 * q + 3 + m // 2)
                    else:
                        pe.wait_ge(dn_ev, 8 * q + m - 3)
                    for h in range(2):
                        last = down_half(slot(m % 4, *span(h)), m, h, gs)
                    last.then_inc(w_used if m % 4 == 3 else dn_mm, 1)

            def down_half(out, m, h, gs):
                for k in range(2):
                    c = (m // 4) * CH + ((m % 4) * 2 + k) * P
                    last = three(out, w_hi[:, c:c + P], w_lo[:, c:c + P],
                                 tile(cv_r, gs + k, *span(h)), tile(ga_r, gs + k, *span(h)), k == 0, k == 1)
                return last

            first_pair(N_FFN, 0, lambda h, k: (n2["lo"], h * KT + k + 1))
            up(1, 1, N_FFN + 2, None)

            def ffn(i):
                n = N_FFN + UPC + 12 * i
                for s in range(2):
                    up(4 * i + 2 + s, s, n + 2 * s, None if isinstance(i, int) else 16 * i - 3)
                down(2 * i, n + 4, 0)
                for s in range(2):
                    up(4 * i + 4 + s, s, n + 6 + 2 * s, 16 * i + 5)
                down(2 * i + 1, n + 10, 2)
            ffn(0)
            with pe.Fori(1, STEPS // 2) as i:
                ffn(i)

            q, n = STEPS - 1, NCHUNKS - 2
            pe.wait_ge(f_lo, 2 * q + 2)
            pe.wait_ge(w_split, n + 2)
            pe.wait_ge(dn_ev, 8 * q)

            def statistics(h):
                z = nf[h]
                pe.wait_ge(z["sum"], KT)
                sum_positions(bank(6), nf_sum, 4, z["ss"])

            def broadcast(h):
                z = nf[h]
                pe.wait_ge(z["diag"], 4)
                if h:
                    pe.wait_ge(nf[0]["out"], KT)
                nc.tensor.matmul(bank(7), ones[:, :], nf_diag, start=True, stop=True).then_inc(z["bc"], 1)

            for h in range(2):
                for m in range(KT):
                    t = h * KT + m
                    wait(pe, x2_done, t - 5)
                    down_half(bank(t % 6), m, h, 0).then_inc(x2_mm, 1)
                    if h and m == 2:
                        statistics(0)
                    if h and m == 4:
                        broadcast(0)
            statistics(1)
            broadcast(1)


def lay_out(np, x, w_in, b_in, conv_dw_w, conv_dw_b, conv_ln_g, conv_ln_b, conv_w_out, pool_w, pool_scale,
            mix_w_out, norm_mix, ffn_w_up, ffn_dw_w, ffn_dw_b, ffn_w_down, norm_ffn, norm_final):
    def block_tiles(w):
        k, n = w.shape
        return w.reshape(k // P, P, n // P, P).transpose(2, 1, 0, 3).reshape(n // P, P, k)

    parts = {kind: block_tiles(w_in[0][:, i * DM:(i + 1) * DM]) for kind, i in _part.items()}
    chunks = [parts[kind][i] for kind, i in in_order() if kind != "m"]
    chunks += list(block_tiles(conv_w_out[0])) + list(block_tiles(mix_w_out[0]))
    up = block_tiles(ffn_w_up[0])
    dn = ffn_w_down[0].reshape(STEPS, CHUNK_PAIRS, P, 2, 4, P).transpose(0, 3, 2, 4, 1, 5).reshape(STEPS, 2, P, CH)

    def ups(q):
        return [t for p in range(CHUNK_PAIRS * q, CHUNK_PAIRS * (q + 1)) for t in (up[p], up[p + FT])]

    chunks += ups(0)
    for q in range(1, STEPS):
        chunks += ups(q) + list(dn[q - 1])
    chunks += list(dn[STEPS - 1])
    stream = np.ascontiguousarray(np.concatenate(chunks, axis=0))

    def per_channel(v):
        return v.reshape(-1, P).T

    edge = np.zeros((NG, WPAD), np.float32)
    for g, w in enumerate(WINDOWS):
        edge[g] = w / np.minimum(np.arange(1, WPAD + 1), w)
    params = np.ascontiguousarray(np.concatenate([
        per_channel(b_in[0]),
        conv_dw_w[0].reshape(TAPS, KT, P).transpose(2, 1, 0).reshape(P, KT * TAPS),
        per_channel(conv_dw_b[0]), per_channel(conv_ln_g[0]), per_channel(conv_ln_b[0]), per_channel(pool_scale[0]),
        per_channel(norm_mix[0]), per_channel(norm_ffn[0]), per_channel(norm_final),
        ffn_dw_w[0].reshape(3, 2 * FT, P).transpose(2, 1, 0).reshape(P, 2 * FT * 3),
        per_channel(ffn_dw_b[0]), np.broadcast_to(edge.reshape(1, -1), (P, NG * WPAD)),
    ], axis=1))
    pw = np.ascontiguousarray(pool_w[0].reshape(NG, 2, P, 2, P).transpose(2, 0, 1, 3, 4).reshape(P, 2 * CH))
    return {"xT": np.ascontiguousarray(x[0].T), "wstream": stream, "pool_w": pw, "params": params}


def kernel(**inputs):
    import numpy as np
    import concourse.bacc as bacc
    from concourse import mybir
    from concourse.bass_utils import run_bass_kernel_spmd

    arrays = lay_out(np, **{k: np.asarray(v) for k, v in inputs.items()})
    nc = bacc.Bacc("TRN2", target_bir_lowering=False, num_devices=1)
    args = [nc.dram_tensor(f"in_{n}", arrays[n].shape, mybir.dt.float32, kind="ExternalInput").ap()
            for n in ("xT", "wstream", "pool_w", "params")]
    out = nc.dram_tensor("outT", (DM, SEQ), mybir.dt.float32, kind="ExternalOutput").ap()
    build(nc, *args, out)
    r = run_bass_kernel_spmd(nc, [{f"in_{n}": a for n, a in arrays.items()}], core_ids=[0])
    return np.ascontiguousarray(r.results[0]["outT"].T)[None]
```

```python
EPS = 1e-6
P = 128
SEQ = 1024
HALF = SEQ // 2
PARTS = 4
PART = SEQ // PARTS
DM = 1024
KT = DM // P
TAPS = 31
PAD = TAPS - 1
WINDOWS = (2, 4, 8, 16)
NG = len(WINDOWS)
WPAD = max(WINDOWS)
D_FF = 2816
FT = D_FF // P
CH = 8 * P
CHUNK_PAIRS = 2
STEPS = FT // CHUNK_PAIRS

_cols = {}
_n = 0
for _name, _w in (("norm_mix", KT), ("b_in", 5 * KT), ("conv_w", KT * TAPS), ("conv_b", KT), ("ln_g", KT),
                  ("ln_b", KT), ("scale", KT), ("norm_ffn", KT), ("norm_final", KT),
                  ("ffn_w", 2 * FT * 3), ("ffn_b", 2 * FT), ("edge", NG * WPAD)):
    _cols[_name] = _n
    _n += _w
NPAR = _n

START = tuple((x[0], int(x[1])) for x in (
    "v0 g0 v1 g1 p0 p1 v2 g2 p2 p3 m0 v3 g3 p4 p5 m1 v4 g4 p6 p7 v5 g5 m2 b0 b1 v6 g6 m3 a0 a1 v7 g7").split())
PAIR0 = 2

_part = {"v": 0, "g": 1, "p": 2, "a": 3, "b": 4}


def in_order():
    return list(START) + [(k, c) for c in range(PAIR0, KT) for k in "ab"]


CHUNK, TURN = {}, {}
for _kind, _i in in_order():
    if _kind != "m":
        CHUNK[_kind, _i] = len(CHUNK)
    if _kind != "v":
        TURN[_kind, _i] = sum(2 if k == "m" else 1 for k, _ in TURN)
N_PAIRS, T_PAIRS = CHUNK["a", PAIR0] - 2 * PAIR0, TURN["a", PAIR0] - 2 * PAIR0
N_OUT = 5 * KT
N_MIX = N_OUT + KT
N_FFN = N_MIX + KT
UPC = 2 * CHUNK_PAIRS
DNC = 2
NCHUNKS = N_FFN + STEPS * (UPC + DNC)

BESIDE = {2: ["glu0"], 4: ["w0", "w1"], 5: ["glu1"], 8: ["lo0", "cs0"], 9: ["glu2"], 12: ["lo1", "cs1", "w2"],
          13: ["glu3"], 16: ["lo2", "cs2", "w3"], 17: ["glu4"], 20: ["cs3"], 21: ["lo3"], 22: ["glu5", "gb0"],
          23: ["gb1"], 25: ["glu6", "cs4"], 28: ["cs5"], 29: ["glu7"], 32: ["cs6"]}
for _c in range(PAIR0, KT):
    BESIDE.setdefault(N_PAIRS + 2 * _c + 3, []).append(f"gb{_c}")


def build(nc, xT, wstream, pool_w, params, outT):
    import concourse.bass as bass
    from concourse import mybir
    from contextlib import ExitStack

    f32, f32r = mybir.dt.float32, mybir.dt.float32r
    ACT = mybir.ActivationFunctionType
    ALU = mybir.AluOpType

    MEAN_AT = 5
    SUMMED1 = 4
    FINAL = ((0, HALF), (HALF, HALF + PART), (HALF + PART, SEQ))
    LAST_SQUARES = 2
    STATS_AT = {1: 4, 2: 3}
    BY_POOL = 2

    ctx = ExitStack()
    with ctx:
        def sb(name, cols, dt=f32):
            return ctx.enter_context(nc.sbuf_tensor(name, [P, cols], dt))

        def two_views(name_f32, name_f32r, cols):
            with nc.sbuf_tensor(name_f32, [P, cols], f32) as plain:
                pass
            return plain, sb(name_f32r, cols, f32r)

        def sem(name):
            return ctx.enter_context(nc.semaphore(name))

        def sems(*names):
            return [sem(n) for n in names]

        TS = KT * SEQ
        h_hi, h_lo = sb("h_hi", TS, f32r), sb("h_lo", TS, f32r)
        res = sb("res", TS)
        cv, cv_r = two_views("cv", "cv_r", TS)
        ga, ga_r = two_views("ga", "ga_r", TS)
        raw = sb("raw", 2 * CH)
        w_hi, w_lo = sb("w_hi", 2 * CH, f32r), sb("w_lo", 2 * CH, f32r)
        GLW = PAD + SEQ + 2
        tmp = sb("tmp", 2 * GLW + 2 * SEQ + WPAD)
        par = sb("par", NPAR)
        ones, ident = sb("ones", P), sb("ident", P)
        eps = sb("eps", 1)
        small = sb("small", 64)
        mean_w = sb("mean_w", P)
        ps = ctx.enter_context(nc.psum_tensor("ps", [P, 4 * SEQ], f32))

        def slot(n, a=0, b=SEQ):
            return ps[:, n * SEQ + a:n * SEQ + b]

        def bank(n, a=0, b=HALF):
            return ps[:, n * HALF + a:n * HALF + b]

        def tile(t, i, a=0, b=SEQ):
            return t[:, bass.ds(i * SEQ + a, b - a)]

        def span(h):
            return h * HALF, (h + 1) * HALF

        def part(p):
            return p * PART, (p + 1) * PART

        def par1(name, i):
            return par[:, bass.ds(i + _cols[name], 1)]

        csum = tmp[:, 2 * GLW:2 * GLW + SEQ]
        sgb = tmp[:, 2 * GLW + SEQ:2 * GLW + 2 * SEQ]

        def glu(c, a, n=SEQ):
            return tmp[:, bass.ds((c % 2) * GLW + a, n)]

        sq = [tmp[:, i * GLW:i * GLW + SEQ] for i in range(2)]
        acc_a = [tmp[:, i * SEQ:(i + 1) * SEQ] for i in range(2)]
        acc_b = [tmp[:, (2 + i) * SEQ:(3 + i) * SEQ] for i in range(2)]
        diag = tmp[:, 0:SEQ]
        nt = [tmp[:, 2 * GLW + i * HALF:2 * GLW + (i + 1) * HALF] for i in (0, 2, 3, 1)]
        n1_sq = [[t[:, i * PART:(i + 1) * PART] for i in range(KT)] for t in (tmp, cv)]
        n1_nt = [[cv[:, i * PART:(i + 1) * PART] for i in range(n, n + 4)] for n in (8, 12)]
        n1_diag = [cv[:, i * PART:(i + 1) * PART] for i in range(16, 16 + PARTS)]
        nf_sq = [tmp[:, i * HALF:(i + 1) * HALF] for i in range(3)]
        nf_sum = [tmp[:, (3 + i) * HALF:(4 + i) * HALF] for i in range(2)]
        nf_diag = [tmp[:, a + 5 * HALF:b + 5 * HALF] for a, b in FINAL]
        nf_scale = tmp[:, 7 * HALF:7 * HALF + PART]

        def nf_square(f, m):
            return nf_sq[(f * KT + m) % 3][:, 0:FINAL[f][1] - FINAL[f][0]]

        XW = WPAD + SEQ
        px = [cv[:, 6 * SEQ:6 * SEQ + XW], ga[:, 6 * SEQ:6 * SEQ + XW]]
        pst = [tmp[:, 2 * GLW + SEQ:2 * GLW + SEQ + XW], res[:, 6 * SEQ:6 * SEQ + XW]]
        pw_raw = res[:, 4 * SEQ:6 * SEQ]
        pp_hi = [ga_r[:, i * SEQ:(i + 1) * SEQ] for i in range(2)]
        pp_lo = [ga_r[:, (2 + i) * SEQ:(3 + i) * SEQ] for i in range(2)]
        GW = 4 * P
        pw_hi = [ga_r[:, (4 + i) * SEQ:(4 + i) * SEQ + GW] for i in range(2)]
        pw_lo = [ga_r[:, (4 + i) * SEQ + GW:(4 + i) * SEQ + 2 * GW] for i in range(2)]

        gain_loaded, par_loaded, pw_loaded, out_stored = sems("gain_loaded", "par_loaded", "pw_loaded", "out_stored")
        xre_loaded = sem("xre_loaded")
        x_loaded = [[sem(f"x_loaded{p}{q}") for q in range(2 if p == 0 else 1)] for p in range(PARTS)]
        raw_loaded = [sem(f"raw_loaded{s}") for s in range(2)]
        split_go, w_hi_done, w_split, w_used = sems("split_go", "w_hi_done", "w_split", "w_used")
        consts, act_go, root_ready = sems("consts", "act_go", "root_ready")
        inverted = sem("inverted")
        s1_half, s1_out, pool_mm = sems("s1_half", "s1_out", "pool_mm")
        n1 = [{n: sem(f"n1_{p}_{n}") for n in ("sq_a", "var", "std", "diag", "bc", "val", "hi", "lo_v") + extra}
              for p, extra in enumerate((("sum", "sq_v"), ("sum",)) + (PARTS - 2) * (("sum", "lo_p"),))]
        pads, sums, pw_hi_done, pw_lo_done, p_mean, p_hi, p_lo = sems(
            "pads", "sums", "pw_hi_done", "pw_lo_done", "p_mean", "p_hi", "p_lo")
        val_out, glu_done, conv_tap, conv_last, cv_done, cs_done, gb_done = sems(
            "val_out", "glu_done", "conv_tap", "conv_last", "cv_done", "cs_done", "gb_done")
        ln = {n: sem("ln_" + n) for n in ("mean", "d", "sq", "sum", "var", "std", "diag", "bc", "n", "z")}
        z_hi, z_lo = sems("z_hi", "z_lo")
        co_a, co_m, co_hi, co_lo = sems("co_a", "co_m", "co_hi", "co_lo")
        x1_done, mix_half = sems("x1_done", "mix_half")
        n2_sq, n2_sum = sems("n2_sq", "n2_sum")
        n2 = [{n: sem(f"n2_{h}_{n}") for n in ("var", "std", "diag", "bc", "val", "hi", "lo_v", "lo_p")} for h in range(2)]
        f_acca, f_accb, f_ca1, f_ca, f_cb1, f_cb, f_gelu, f_g, f_hi, f_lo, dn_mm, dn_ev = sems(
            "f_acca", "f_accb", "f_ca1", "f_ca", "f_cb1", "f_cb", "f_gelu", "f_g", "f_hi", "f_lo", "dn_mm", "dn_ev")
        x2_mm, x2_done, last_gain, last_scale, last_out = sems("x2_mm", "x2_done", "last_gain", "last_scale", "last_out")
        nf = [{n: sem(f"nf_{h}_{n}") for n in ("sq", "sum", "var", "std", "diag", "bc", "out")} for h in range(len(FINAL))]

        block = ctx.enter_context(nc.Block())

        def wait(eng, s, v):
            if not (isinstance(v, int) and v <= 0):
                eng.wait_ge(s, v)

        def out_of(turn):
            return 2 * turn + 2

        @block.sync
        def _(sp):
            x_s, x_d = res[:, :].rearrange("p (k n) -> p k n", k=KT), xT.rearrange("(k p) n -> p k n", p=P)
            def load_x(p):
                n, (a, b) = len(x_loaded[p]), part(p)
                for q in range(n):
                    k = slice(KT // n * q, KT // n * (q + 1))
                    sp.dma_start(x_s[:, k, a:b], x_d[:, k, a:b]).then_inc(x_loaded[p][q], 16)

            def load_weights(s):
                sp.dma_start(raw[:, s * CH:(s + 1) * CH], wstream[s * P:(s + 1) * P, :]).then_inc(raw_loaded[s], 16)

            load_x(0)
            sp.dma_start(par[:, 0:KT], params[:, 0:KT]).then_inc(gain_loaded, 16)
            load_weights(0)
            load_x(1)
            load_weights(1)
            load_x(2)
            load_x(3)
            sp.dma_start(par[:, KT:], params[:, KT:]).then_inc(par_loaded, 16)
            with sp.Fori(1, NCHUNKS // 2) as i:
                for s in range(2):
                    sp.wait_ge(w_split, 2 * i + s - 1)
                    sp.dma_start(raw[:, s * CH:(s + 1) * CH],
                                 wstream[bass.ds((2 * i + s) * P, P), :]).then_inc(raw_loaded[s], 16)
            o_d = outT.rearrange("(k p) n -> p k n", p=P)
            def store(f, k0, k1, done, n):
                a, b = FINAL[f]
                sp.wait_ge(done, n)
                sp.dma_start(o_d[:, k0:k1, a:b], x_s[:, k0:k1, a:b]).then_inc(out_stored, 16)

            for k in range(2, KT + 1, 2):
                store(0, k - 2, k, nf[0]["out"], k)
            for f in (1, 2):
                for k in (3, KT - BY_POOL):
                    store(f, k - 3, k, nf[f]["out"], k)
                store(f, KT - BY_POOL, KT, last_out, BY_POOL * f)
            sp.wait_ge(out_stored, 16 * 10)

        @block.gpsimd
        def _(pool):
            pool.memset(mean_w[:, :], 1.0 / DM).then_inc(consts, 1)
            pool.memset(eps[:, :], EPS).then_inc(consts, 1)
            pool.memset(ones[:, :], 1.0).then_inc(consts, 1)
            pool.memset(ident[:, :], 0.0).then_inc(consts, 1)
            pool.wait_ge(consts, 4)
            pool.affine_select(out=ident[:, :], in_=ident[:, :], compare_op=ALU.not_equal, fill=1.0,
                               base=0, pattern=[[-1, P]], channel_multiplier=1).then_inc(consts, 1)

            def split(n, s, i):
                pool.wait_ge(raw_loaded[s], 16 * (i + 1))
                wait(pool, w_used, n - 1)
                pool.sem_inc(split_go, 1)
                r, hi, lo = (t[:, s * CH:(s + 1) * CH] for t in (raw, w_hi, w_lo))
                pool.tensor_scalar(hi, r, 1.0, 0.0, ALU.mult, ALU.add).then_inc(w_hi_done, 1)
                pool.wait_ge(w_hi_done, n + 1)
                pool.tensor_tensor(lo, r, hi.bitcast(f32), ALU.subtract).then_inc(w_split, 1)

            def beside(what, i):
                if what == "glu":
                    pool.wait_ge(val_out, i + 1)
                    pool.wait_ge(s1_out, out_of(TURN["g", i]))
                    if i == 0:
                        pool.wait_ge(pads, 3)
                    pool.tensor_tensor(glu(i, PAD), glu(i, PAD), tile(cv, i), ALU.mult).then_inc(glu_done, 1)
                if what == "cs":
                    pool.wait_ge(cv_done, i + 1)
                    wait(pool, cs_done, i)
                    pool.tensor_tensor(csum, csum, tile(cv, i), ALU.add).then_inc(cs_done, 1)
                if what == "gb":
                    pool.wait_ge(s1_out, out_of(TURN["b", i]))
                    pool.tensor_tensor(tile(res, i), sgb, tile(res, i), ALU.mult).then_inc(gb_done, 1)
                if what == "lo":
                    wait(pool, pool_mm, 2 * i)
                    for j in range(2):
                        pool.wait_ge(p_hi, 2 * i + j + 1)
                        pool.tensor_tensor(pp_lo[j], px[j][:, WPAD:], pp_hi[j].bitcast(f32), ALU.subtract).then_inc(p_lo, 1)
                if what == "w":
                    pool.wait_ge(pw_loaded, 16)
                    wait(pool, pool_mm, 2 * (i - 1))
                    r = pw_raw[:, i * GW:(i + 1) * GW]
                    pool.tensor_scalar(pw_hi[i % 2], r, 1.0, 0.0, ALU.mult, ALU.add).then_inc(pw_hi_done, 1)
                    pool.wait_ge(pw_hi_done, i + 1)
                    pool.tensor_tensor(pw_lo[i % 2], r, pw_hi[i % 2].bitcast(f32), ALU.subtract).then_inc(pw_lo_done, 1)

            LOOSE = max(BESIDE) // 2 + 1
            for n in range(2):
                split(n, n, 0)
            def low_halves(z, a, b, bufs):
                for k in range(1, KT, 2):
                    pool.wait_ge(z["hi"], k + 1)
                    pool.tensor_tensor(tile(h_lo, k, a, b), bufs[k % 4], tile(h_hi, k, a, b).bitcast(f32),
                                       ALU.subtract).then_inc(z["lo_p"], 1)

            for p in range(1, PARTS):
                z, squares = n1[p], n1_sq[p % 2]
                for k in range(SUMMED1 if p == 1 else 1, KT):
                    pool.wait_ge(z["sq_a"], k + 1)
                    wait(pool, z["sum"], k - 1)
                    pool.tensor_tensor(squares[0], squares[0], squares[k], ALU.add).then_inc(z["sum"], 1)
            for p in range(2, PARTS):
                low_halves(n1[p], *part(p), n1_nt[p % 2])
            for n in range(2, 2 * LOOSE):
                split(n, n % 2, n // 2)
                for x in BESIDE.get(n, ()):
                    beside(x[:-1], int(x[-1]))

            def splits(i0, i1):
                with pool.Fori(i0, i1) as i:
                    for s in range(2):
                        split(2 * i + s, s, i)

            splits(LOOSE, N_FFN // 2 + 1)
            for h in range(2):
                low_halves(n2[h], *span(h), nt)
            splits(N_FFN // 2 + 1, NCHUNKS // 2)
            for f in range(len(FINAL)):
                n = FINAL[f][1] - FINAL[f][0]
                total = nf_sum[f % 2][:, 0:n]
                for m in range(1, KT - (LAST_SQUARES if f == 2 else 0)):
                    pool.wait_ge(nf[f]["sq"], m + 1)
                    if m > 1:
                        pool.wait_ge(nf[f]["sum"], m - 1)
                    elif f == 2:
                        pool.wait_ge(nf[0]["var"], 1)
                    pool.tensor_tensor(total, nf_square(f, 0) if m == 1 else total, nf_square(f, m), ALU.add).then_inc(nf[f]["sum"], 1)
            for f in (1, 2):
                pool.wait_ge(nf[f]["sq"], KT)
                last = [tile(res, k, *FINAL[f]) for k in range(KT - BY_POOL, KT)]
                for j in range(BY_POOL):
                    pool.tensor_scalar(last[j], last[j], par1("norm_final", KT - BY_POOL + j), None, ALU.mult).then_inc(last_gain, 1)
                pool.wait_ge(last_scale, f)
                for j in range(BY_POOL):
                    pool.wait_ge(last_gain, BY_POOL * (f - 1) + j + 1)
                    pool.tensor_tensor(last[j], last[j], nf_scale, ALU.mult).then_inc(last_out, 1)

        @block.scalar
        def _(act):
            def deviation(z, std, var, n=HALF // P):
                act.wait_ge(z["var"], 1)
                act.activation(small[:, std:std + n], var[:, 0:n], ACT.Sqrt, bias=eps[:, :]).then_inc(z["std"], 1)

            def root_table():
                act.activation(small[:, 63:64], eps[:, :], ACT.Sqrt).then_inc(root_ready, 1)

            def square1(p, k):
                act.wait_ge(x_loaded[p][k * len(x_loaded[p]) // KT], 16)
                act.activation(n1_sq[p % 2][k], tile(res, k, *part(p)), ACT.Square).then_inc(n1[p]["sq_a"], 1)

            act.wait_ge(consts, 5)
            root_table()
            for k in range(0, KT, 2):
                square1(0, k)
            deviation(n1[0], 0, bank(6), PART // P)
            for k in range(KT):
                square1(1, k)
            for p in range(PARTS):
                for k in range(KT):
                    act.wait_ge(n1[p]["val"], k + 1)
                    act.activation(tile(h_hi, k, *part(p)), n1_nt[p % 2][k % 4], ACT.Copy).then_inc(n1[p]["hi"], 1)
                    if p + 1 < PARTS and k == (KT - 1 if p == 0 else 3):
                        deviation(n1[p + 1], 4 * (p + 1), bank(6 + (p + 1) % 2), PART // P)
                    if p + 2 < PARTS and k >= 3:
                        square1(p + 2, k - 3)
                for k in range(KT - 3, KT):
                    if p + 2 < PARTS:
                        square1(p + 2, k)

            def hold(i):
                if not isinstance(i, int):
                    act.sem_inc(act_go, 1)

            act.wait_ge(n1[-1]["lo_v"], KT // 2)
            act.wait_ge(n1[-1]["lo_p"], KT // 2)
            act.wait_ge(par_loaded, 16)
            act.dma_start(pw_raw, pool_w).then_inc(pw_loaded, 16)

            def read_out(turn, second, second_val, out_ap, func, **kw):
                for h in range(2):
                    act.wait_ge(*((s1_half, turn + 1) if h == 0 else (second, second_val)))
                    hold(turn)
                    act.activation(out_ap[:, h * HALF:(h + 1) * HALF], slot(1, *span(h)), func, **kw).then_inc(s1_out, 1)

            def value(c, n):
                act.wait_ge(w_used, n + 1)
                if c == 0:
                    act.wait_ge(pads, 3)
                wait(act, cv_done, c - 1)
                act.activation(glu(c, PAD), slot(0), ACT.Identity, bias=par1("b_in", c)).then_inc(val_out, 1)

            def gate(c, turn, n):
                if c == 6:
                    act.wait_ge(p_lo, 2 * NG)
                read_out(turn, w_used, n + 1, tile(cv, c), ACT.Sigmoid, bias=par1("b_in", KT + c))

            def gate_a(c, turn, n):
                read_out(turn, w_used, n + 1, tile(ga, c), ACT.Sigmoid, bias=par1("b_in", 3 * KT + c))

            def gate_b(c, turn, n):
                wait(act, gb_done, c)
                if isinstance(c, int) and c == 0:
                    act.wait_ge(p_mean, 2 * NG)
                read_out(turn, w_used, n + 1, sgb, ACT.Sigmoid, bias=par1("b_in", 4 * KT + c))

            def pool_in(t, turn, n):
                wait(act, p_lo, 2 * (t // 2))
                read_out(turn, w_used, n + 1, px[t % 2][:, WPAD:], ACT.Identity, bias=par1("b_in", 2 * KT + t))

            def pool_hi(g):
                for j in range(2):
                    act.wait_ge(p_mean, 2 * g + j + 1)
                    wait(act, pool_mm, 2 * g)
                    act.activation(pp_hi[j], px[j][:, WPAD:], ACT.Copy).then_inc(p_hi, 1)

            def pool_out(g, turn):
                for m in range(2):
                    read_out(turn + m, pool_mm, 2 * g + m + 1, tile(res, 2 * g + m), ACT.Copy, scale=par1("scale", 2 * g + m))

            handlers = {"g": gate, "a": gate_a, "b": gate_b, "p": pool_in}
            hi_after = {("p", 1): 0, ("m", 0): 1, ("m", 1): 2, ("m", 2): 3}
            for kind, i in START:
                if kind == "m":
                    pool_out(i, TURN[kind, i])
                elif kind == "v":
                    value(i, CHUNK[kind, i])
                else:
                    handlers[kind](i, TURN[kind, i], CHUNK[kind, i])
                if (kind, i) in hi_after:
                    pool_hi(hi_after[kind, i])

            def gate_pair(c):
                gate_a(c, 2 * c + T_PAIRS, 2 * c + N_PAIRS)
                gate_b(c, 2 * c + T_PAIRS + 1, 2 * c + N_PAIRS + 1)

            with act.Fori(PAIR0, MEAN_AT) as c:
                gate_pair(c)

            def ln_squares(c0, c1):
                for c in range(c0, c1):
                    act.wait_ge(ln["d"], c + 1)
                    wait(act, ln["sum"], c - 1)
                    act.activation(sq[c % 2], tile(cv, c), ACT.Square).then_inc(ln["sq"], 1)

            ln_squares(0, 4)
            gate_a(MEAN_AT, 2 * MEAN_AT + T_PAIRS, 2 * MEAN_AT + N_PAIRS)
            ln_squares(4, KT)
            gate_b(MEAN_AT, 2 * MEAN_AT + T_PAIRS + 1, 2 * MEAN_AT + N_PAIRS + 1)
            deviation(ln, 16, slot(3), KT)

            def ln_silu(c0, c1):
                for c in range(c0, c1):
                    act.wait_ge(ln["n"], c + 1)
                    act.activation(tile(cv, c), tile(cv, c), ACT.Silu, bias=par1("ln_b", c), scale=par1("ln_g", c)).then_inc(ln["z"], 1)

            gate_a(MEAN_AT + 1, 2 * (MEAN_AT + 1) + T_PAIRS, 2 * (MEAN_AT + 1) + N_PAIRS)
            ln_silu(0, 3)
            gate_b(MEAN_AT + 1, 2 * (MEAN_AT + 1) + T_PAIRS + 1, 2 * (MEAN_AT + 1) + N_PAIRS + 1)
            ln_silu(3, 6)
            gate_a(KT - 1, 2 * (KT - 1) + T_PAIRS, 2 * (KT - 1) + N_PAIRS)
            ln_silu(6, KT)
            act.wait_ge(gb_done, KT - 1)
            turn = TURN["b", KT - 1]
            for h in range(2):
                act.wait_ge(*((s1_half, turn + 1) if h == 0 else (w_used, N_OUT)))
                act.activation(sgb[:, h * HALF:(h + 1) * HALF], slot(1, *span(h)), ACT.Sigmoid,
                               bias=par1("b_in", 5 * KT - 1)).then_inc(s1_out, 1)
                for c in range(KT):
                    if h == 0:
                        act.wait_ge(ln["z"], c + 1)
                    act.activation(tile(h_hi, c, *span(h)), tile(cv, c, *span(h)), ACT.Copy).then_inc(z_hi, 1)

            act.wait_ge(z_lo, 2 * KT)
            xr = xT.rearrange("(k p) n -> p k n", p=P)
            with act.Fori(0, KT // 2) as i:
                for j in range(2):
                    act.wait_ge(co_m, 2 * i + j + 1)
                    act.activation(tile(cv_r, 2 * i + j), tile(res, 2 * i + j), ACT.Copy).then_inc(co_hi, 1)
                act.wait_ge(co_lo, 2 * i + 2)
                act.dma_start(res[:, bass.ds(2 * i * SEQ, 2 * SEQ)].rearrange("p (k n) -> p k n", k=2),
                              xr[:, bass.ds(2 * i, 2), :]).then_inc(xre_loaded, 16)

            act.wait_ge(root_ready, 1)
            root_table()
            for k in range(KT - 1):
                act.wait_ge(x1_done, k + 1)
                wait(act, n2_sum, k - 1)
                act.activation(sq[k % 2], tile(res, k), ACT.Square).then_inc(n2_sq, 1)
            act.wait_ge(n2_sum, KT - 2)
            for h in range(2):
                act.wait_ge(x1_done, KT + h)
                act.activation(sq[(KT - 1) % 2][:, h * HALF:(h + 1) * HALF], tile(res, KT - 1, *span(h)),
                               ACT.Square).then_inc(n2_sq, 1)
            for h in range(2):
                deviation(n2[h], 32 + 8 * h, slot(3, *span(h)))
            for h in range(2):
                for k in range(KT):
                    act.wait_ge(n2[h]["val"], k + 1)
                    act.activation(tile(h_hi, k, *span(h)), nt[k % 4], ACT.Copy).then_inc(n2[h]["hi"], 1)

            def up(p, s, gs, n, dn_need):
                act.wait_ge(w_used, n + 1)
                wait(act, f_g, p - 1)
                act.activation(acc_a[s], slot(2 * s), ACT.Identity, bias=par1("ffn_b", p), scale=par1("ffn_w", p * 3 + 2)).then_inc(f_acca, 1)
                act.wait_ge(f_ca, p + 1)
                act.activation(acc_a[s], acc_a[s], ACT.Gelu_apprx_tanh).then_inc(f_gelu, 1)
                act.wait_ge(w_used, n + 2)
                wait(act, f_lo, p - 1)
                act.activation(acc_b[s], slot(2 * s + 1), ACT.Identity, bias=par1("ffn_b", p + FT), scale=par1("ffn_w", (p + FT) * 3 + 2)).then_inc(f_accb, 1)
                act.wait_ge(f_g, p + 1)
                if dn_need is not None:
                    act.wait_ge(w_used, dn_need)
                act.activation(tile(cv_r, gs), acc_b[s], ACT.Copy).then_inc(f_hi, 1)

            act.wait_ge(n2[1]["lo_v"], KT // 2)
            act.wait_ge(n2[1]["lo_p"], KT // 2)
            up(0, 0, 0, N_FFN, None)
            up(1, 1, 1, N_FFN + 2, None)

            def ffn(i):
                n = N_FFN + UPC + 12 * i
                for s in range(2):
                    up(4 * i + 2 + s, s, 2 + s, n + 2 * s, None if isinstance(i, int) else n)
                for s in range(2):
                    up(4 * i + 4 + s, s, s, n + 6 + 2 * s, n + 6)
            ffn(0)
            with act.Fori(1, STEPS // 2) as i:
                ffn(i)

            act.wait_ge(root_ready, 2)
            root_table()
            for f in range(len(FINAL)):
                for m in range(KT):
                    t = f * KT + m
                    act.wait_ge(x2_done, t + 1)
                    if t >= 3:
                        act.wait_ge(nf[(t - 3) // KT]["sum"], max((t - 3) % KT, 1))
                    act.activation(nf_square(f, m), tile(res, m, *FINAL[f]), ACT.Square).then_inc(nf[f]["sq"], 1)
                    if f and m == STATS_AT[f] + 1:
                        deviation(nf[f - 1], 8 * (f - 1), bank(6, 4 * (f - 1)), (4, 2)[f - 1])
            act.wait_ge(nf[1]["bc"], 2)
            act.activation(nf_scale, bank(1, 0, PART), ACT.Copy).then_inc(last_scale, 1)
            deviation(nf[2], 16, bank(6, 8), 2)
            act.wait_ge(nf[2]["bc"], 2)
            act.wait_ge(last_out, BY_POOL)
            act.activation(nf_scale, bank(3, 0, PART), ACT.Copy).then_inc(last_scale, 1)

        @block.vector
        def _(dve):
            n_inverted = [0]

            def invert(z, std, dst, n=HALF // P):
                dve.wait_ge(z["std"], 1)
                dve.reciprocal(small[:, std + n:std + 2 * n], small[:, std:std + n]).then_inc(inverted, 1)
                n_inverted[0] += 1
                dve.wait_ge(inverted, n_inverted[0])
                for j in range(n):
                    dve.tensor_scalar(dst[:, j * P:(j + 1) * P], ident[:, :], small[:, std + n + j:std + n + j + 1], None,
                                      ALU.mult).then_inc(z["diag"], 1)

            def normed(z, a, b, gain, scales, bufs, shared, at=None, between=None):
                dve.wait_ge(z["bc"], 1)

                def low(k):
                    if shared and k % 2:
                        return
                    dve.wait_ge(z["hi"], k + 1)
                    dve.tensor_tensor(tile(h_lo, k, a, b), bufs[k % 4], tile(h_hi, k, a, b).bitcast(f32),
                                      ALU.subtract).then_inc(z["lo_v"], 1)

                for k in range(KT):
                    if k >= 4:
                        if shared and k % 2:
                            dve.wait_ge(z["lo_p"], k // 2 - 1)
                        else:
                            dve.wait_ge(z["lo_v"], k // 2 - 1 if shared else k - 3)
                    dve.scalar_tensor_tensor(out=bufs[k % 4], in0=tile(res, k, a, b), scalar=par1(gain, k),
                                             in1=scales, op0=ALU.mult, op1=ALU.mult).then_inc(z["val"], 1)
                    if k:
                        low(k - 1)
                    if k == at:
                        between()
                low(KT - 1)

            def settled(z, shared):
                dve.wait_ge(z["lo_v"], KT // 2 if shared else KT)
                if shared:
                    dve.wait_ge(z["lo_p"], KT // 2)

            dve.wait_ge(consts, 5)
            for q in range(2):
                for k in range(4 * q + 1, 4 * q + 4, 2):
                    dve.wait_ge(x_loaded[0][q], 16)
                    dve.tensor_tensor(n1_sq[0][k], tile(res, k, *part(0)), tile(res, k, *part(0)), ALU.mult).then_inc(n1[0]["sq_v"], 1)
                a = 4 * q * PART
                for n in (2, 1):
                    if n == 2:
                        dve.wait_ge(n1[0]["sq_a"], 2 * q + 2)
                        dve.wait_ge(n1[0]["sq_v"], 2 * q + 2)
                    else:
                        dve.wait_ge(n1[0]["sum"], 2 * q + 1)
                    dve.tensor_tensor(tmp[:, a:a + n * PART], tmp[:, a:a + n * PART], tmp[:, a + n * PART:a + 2 * n * PART],
                                      ALU.add).then_inc(n1[0]["sum"], 1)
            dve.wait_ge(n1[0]["sum"], 4)
            dve.tensor_tensor(n1_sq[0][0], n1_sq[0][0], n1_sq[0][4], ALU.add).then_inc(n1[0]["sum"], 1)
            dve.wait_ge(gain_loaded, 16)

            def invert1(p):
                invert(n1[p], 4 * p, n1_diag[p], PART // P)

            invert1(0)
            for k in range(1, SUMMED1):
                dve.wait_ge(n1[1]["sq_a"], k + 1)
                wait(dve, n1[1]["sum"], k - 1)
                dve.tensor_tensor(n1_sq[1][0], n1_sq[1][0], n1_sq[1][k], ALU.add).then_inc(n1[1]["sum"], 1)
            for p in range(PARTS):
                if p >= 2:
                    settled(n1[p - 2], False)
                normed(n1[p], *part(p), "norm_mix", bank(4 + p % 2, 0, PART), n1_nt[p % 2], p >= 2,
                       None if p + 1 == PARTS else 7 if p == 0 else 4, lambda: invert1(p + 1))
            for z in n1[2:]:
                settled(z, True)
            dve.wait_ge(par_loaded, 16)
            for c in range(2):
                dve.memset(glu(c, 0, PAD), 0.0).then_inc(pads, 1)
            dve.memset(csum, 0.0).then_inc(pads, 1)
            for t in px + pst:
                dve.memset(t[:, 0:WPAD], 0.0).then_inc(pads, 1)
            dve.wait_ge(pads, 7)

            def conv(c, between=(), at=None):
                base = c * (TAPS - 1)
                dve.wait_ge(glu_done, c + 1)
                order = [PAD, PAD - 1] + list(range(PAD - 1))
                for n, t in enumerate(order):
                    if n == at:
                        between()
                    acc, w = slot(2 + n % 2), par1("conv_w", c * TAPS + t)
                    if n == 0:
                        wait(dve, cv_done, c)
                        dve.tensor_scalar(acc, glu(c, t), w, par1("conv_b", c), ALU.mult, ALU.add).then_inc(conv_tap, 1)
                    elif n == 1:
                        dve.tensor_scalar(acc, glu(c, t), w, None, ALU.mult).then_inc(conv_tap, 1)
                    else:
                        dve.wait_ge(conv_tap, base + n - 1)
                        last = n == TAPS - 1
                        dve.scalar_tensor_tensor(out=tile(cv, c) if last else acc, in0=glu(c, t), scalar=w, in1=acc,
                                                 op0=ALU.mult, op1=ALU.add).then_inc(conv_last if last else conv_tap, 1)
                dve.wait_ge(conv_last, c + 1)
                dve.tensor_tensor(tile(cv, c), slot(3), tile(cv, c), ALU.add).then_inc(cv_done, 1)

            n_sums = [0]

            def added(ins):
                n_sums[0] += 1
                ins.then_inc(sums, 1)
                dve.wait_ge(sums, n_sums[0])

            def pool_mean(g):
                w = WINDOWS[g]
                for j in range(2):
                    dve.wait_ge(s1_out, out_of(TURN["p", 2 * g + j]))
                    src, d, n = px[j], 1, 0
                    while d < w:
                        added(dve.tensor_tensor(pst[n][:, WPAD:], src[:, WPAD:], src[:, WPAD - d:WPAD - d + SEQ], ALU.add))
                        src, d, n = pst[n], 2 * d, 1 - n
                    e = _cols["edge"] + g * WPAD
                    added(dve.tensor_tensor(src[:, WPAD:2 * WPAD], src[:, WPAD:2 * WPAD], par[:, e:e + WPAD], ALU.mult))
                    dve.scalar_tensor_tensor(out=px[j][:, WPAD:], in0=src[:, WPAD:], scalar=1.0 / w, in1=px[j][:, WPAD:],
                                             op0=ALU.mult, op1=ALU.subtract).then_inc(p_mean, 1)
                    dve.wait_ge(p_mean, 2 * g + j + 1)

            conv(0)
            conv(1, lambda: pool_mean(0), 4)
            for c in range(2, 5):
                pool_mean(c - 1)
                conv(c)
            with dve.Fori(5, KT) as c:
                conv(c)

            dve.wait_ge(cs_done, KT - 1)
            dve.wait_ge(cv_done, KT)
            dve.tensor_tensor(csum, csum, tile(cv, KT - 1), ALU.add).then_inc(cs_done, 1)

            dve.wait_ge(ln["mean"], 2)

            def centre(c):
                dve.tensor_tensor(tile(cv, c), tile(cv, c), slot(2), ALU.subtract).then_inc(ln["d"], 1)

            def add_square(squared, summed, k):
                dve.wait_ge(squared, k + 1)
                wait(dve, summed, k)
                if k == 0:
                    dve.tensor_copy(csum, sq[0]).then_inc(summed, 1)
                else:
                    dve.tensor_tensor(csum, csum, sq[k % 2], ALU.add).then_inc(summed, 1)

            for c in range(KT):
                centre(c)
                if c:
                    add_square(ln["sq"], ln["sum"], c - 1)
            add_square(ln["sq"], ln["sum"], KT - 1)
            invert(ln, 16, diag, KT)
            dve.wait_ge(ln["bc"], 1)
            for c in range(KT):
                dve.tensor_tensor(tile(cv, c), tile(cv, c), slot(2), ALU.mult).then_inc(ln["n"], 1)
            for h in range(2):
                for c in range(KT):
                    dve.wait_ge(z_hi, h * KT + c + 1)
                    dve.tensor_tensor(tile(h_lo, c, *span(h)), tile(cv, c, *span(h)), tile(h_hi, c, *span(h)).bitcast(f32),
                                      ALU.subtract).then_inc(z_lo, 1)

            dve.wait_ge(s1_out, out_of(TURN["a", KT - 1]))
            dve.wait_ge(gb_done, KT)
            with dve.Fori(0, KT // 2) as i:
                for j in range(2):
                    m = 2 * i + j
                    dve.wait_ge(w_used, N_OUT + m + 1)
                    dve.tensor_tensor(tile(ga, m), slot(j), tile(ga, m), ALU.mult).then_inc(co_a, 1)
                    dve.wait_ge(co_a, m + 1)
                    dve.tensor_tensor(tile(res, m), tile(ga, m), tile(res, m), ALU.add).then_inc(co_m, 1)
                    dve.wait_ge(co_hi, m + 1)
                    dve.tensor_tensor(tile(ga_r, m), tile(res, m), tile(cv_r, m).bitcast(f32), ALU.subtract).then_inc(co_lo, 1)

            dve.wait_ge(xre_loaded, 16 * (KT // 2))
            for m in range(KT - 1):
                dve.wait_ge(w_used, N_MIX + m + 1)
                dve.tensor_tensor(tile(res, m), slot(m % 2), tile(res, m), ALU.add).then_inc(x1_done, 1)
                if m:
                    add_square(n2_sq, n2_sum, m - 1)
            for h in range(2):
                dve.wait_ge(*((mix_half, 1) if h == 0 else (w_used, N_FFN)))
                dve.tensor_tensor(tile(res, KT - 1, *span(h)), slot((KT - 1) % 2, *span(h)), tile(res, KT - 1, *span(h)),
                                  ALU.add).then_inc(x1_done, 1)
                if h == 0:
                    add_square(n2_sq, n2_sum, KT - 2)
                else:
                    invert(n2[0], 32, diag[:, 0:HALF])
                dve.wait_ge(n2_sq, KT + h)
                dve.wait_ge(n2_sum, KT - 1)
                a, b = span(h)
                dve.tensor_tensor(csum[:, a:b], csum[:, a:b], sq[(KT - 1) % 2][:, a:b], ALU.add).then_inc(n2_sum, 1)
            for h in range(2):
                normed(n2[h], *span(h), "norm_ffn", slot(2, *span(h)), nt, True, None if h else 1,
                       lambda: invert(n2[1], 40, diag[:, HALF:SEQ]))
                settled(n2[h], True)

            def up(p, s, gs):
                for f, acc, started, first_tap, done, n in ((p, acc_a[s], f_acca, f_ca1, f_ca, 2 * s),
                                                            (p + FT, acc_b[s], f_accb, f_cb1, f_cb, 2 * s + 1)):
                    dve.wait_ge(started, p + 1)
                    for d, s_done in ((1, first_tap), (2, done)):
                        dve.scalar_tensor_tensor(out=acc[:, d:], in0=slot(n, 0, SEQ - d), scalar=par1("ffn_w", f * 3 + 2 - d),
                                                 in1=acc[:, d:], op0=ALU.mult, op1=ALU.add).then_inc(s_done, 1)
                        if d == 1:
                            dve.wait_ge(s_done, p + 1)
                dve.wait_ge(f_gelu, p + 1)
                dve.wait_ge(f_cb, p + 1)
                dve.tensor_tensor(acc_b[s], acc_a[s], acc_b[s], ALU.mult).then_inc(f_g, 1)
                dve.wait_ge(f_hi, p + 1)
                dve.tensor_tensor(tile(ga_r, gs), acc_b[s], tile(cv_r, gs).bitcast(f32), ALU.subtract).then_inc(f_lo, 1)

            def down(q, n):
                for m in range(KT):
                    if m % 4 == 3:
                        dve.wait_ge(w_used, n + m // 4 + 1)
                    else:
                        dve.wait_ge(dn_mm, 6 * q + m - m // 4 + 1)
                    wait(dve, dn_ev, 8 * q + m)
                    dve.tensor_tensor(tile(res, m), slot(m % 4), tile(res, m), ALU.add).then_inc(dn_ev, 1)

            for s in range(2):
                up(s, s, s)

            def ffn(i):
                n = N_FFN + UPC + 12 * i
                for s in range(2):
                    up(4 * i + 2 + s, s, 2 + s)
                down(2 * i, n + 4)
                for s in range(2):
                    up(4 * i + 4 + s, s, s)
                down(2 * i + 1, n + 10)
            ffn(0)
            with dve.Fori(1, STEPS // 2) as i:
                ffn(i)

            dve.wait_ge(dn_ev, 8 * (STEPS - 1))

            def last_add(f, m):
                dve.wait_ge(x2_mm, f * KT + m + 1)
                t = tile(res, m, *FINAL[f])
                dve.tensor_tensor(t, bank((f * KT + m) % 6, 0, FINAL[f][1] - FINAL[f][0]), t, ALU.add).then_inc(x2_done, 1)

            def final(f, k):
                if k == 0:
                    dve.wait_ge(nf[f]["bc"], 1)
                t = tile(res, k, *FINAL[f])
                dve.scalar_tensor_tensor(out=t, in0=t, scalar=par1("norm_final", k),
                                         in1=bank((7, 0, 2)[f], 0, FINAL[f][1] - FINAL[f][0]),
                                         op0=ALU.mult, op1=ALU.mult).then_inc(nf[f]["out"], 1)

            for m in range(KT):
                last_add(0, m)
            for m in range(KT):
                last_add(1, m)
                if m == STATS_AT[1] + 1:
                    invert(nf[0], 0, nf_diag[0], 4)
            for m in range(KT):
                last_add(2, m)
                if m < 5:
                    final(0, m)
                if m == STATS_AT[2] + 1:
                    invert(nf[1], 8, nf_diag[1], 2)
            for k in range(5, 6):
                final(0, k)
            for m in range(KT - LAST_SQUARES, KT):
                dve.wait_ge(nf[2]["sq"], m + 1)
                dve.wait_ge(nf[2]["sum"], m - 1)
                total = nf_sum[0][:, 0:PART]
                dve.tensor_tensor(total, total, nf_square(2, m), ALU.add).then_inc(nf[2]["sum"], 1)
            for k in range(6, 7):
                final(0, k)
            invert(nf[2], 16, nf_diag[2], 2)
            for k in range(7, KT):
                final(0, k)
            for f in (1, 2):
                for k in range(KT - BY_POOL):
                    final(f, k)

        @block.tensor
        def _(pe):
            def three(out, a_hi, a_lo, b_hi, b_lo, start, stop):
                nc.tensor.matmul(out, a_hi, b_lo, start=start, stop=False)
                nc.tensor.matmul(out, a_lo, b_hi, start=False, stop=False)
                return nc.tensor.matmul(out, a_hi, b_hi, start=False, stop=stop)

            def half_tile(s, out, h, mov_hi, mov_lo, ready=None):
                for k in range(KT):
                    if ready:
                        pe.wait_ge(*ready(h, k))
                    c = s * CH + k * P
                    last = three(out, w_hi[:, c:c + P], w_lo[:, c:c + P],
                                 tile(mov_hi, k, *span(h)), tile(mov_lo, k, *span(h)), k == 0, k == KT - 1)
                return last

            def project(n, s, dst, mov_hi, mov_lo, ready=None, half_sem=None):
                pe.wait_ge(w_split, n + 1)
                for h in range(2):
                    last = half_tile(s, slot(dst, *span(h)), h, mov_hi, mov_lo, ready)
                    if h or half_sem:
                        last.then_inc(w_used if h else half_sem, 1)

            def pair_part(n, dst, a, b, ready, used=None, half_sem=None, between={}):
                blocks = [(k, j) for k in range(KT) for j in range(2)]
                if used:
                    blocks.sort(key=lambda kj: kj[1])
                for k, j in blocks:
                    if j == 0:
                        if k in between:
                            between[k]()
                        pe.wait_ge(*ready(k))
                    if a == 0 and k == 0:
                        pe.wait_ge(w_split, n + j + 1)
                    c = ((n + j) % 2) * CH + k * P
                    last = three(slot(dst + j, a, b), w_hi[:, c:c + P], w_lo[:, c:c + P],
                                 tile(h_hi, k, a, b), tile(h_lo, k, a, b), k == 0, k == KT - 1)
                    if k == KT - 1 and used:
                        last.then_inc(used, 1)
                    elif k == KT - 1 and j and half_sem:
                        last.then_inc(half_sem, 1)

            def mean_of(dst, src, wait_for, done):
                pe.wait_ge(*wait_for)
                nc.tensor.matmul(dst, mean_w[:, :], src, start=True, stop=True).then_inc(done, 1)

            def variance(dst, srcs, done, n=HALF // P):
                for wait_for, _ in srcs:
                    pe.wait_ge(*wait_for)
                for j in range(n):
                    for i, (_, src) in enumerate(srcs):
                        last = nc.tensor.matmul(dst[:, j:j + 1], src[:, j * P:(j + 1) * P], mean_w[:, 0:1],
                                                start=i == 0, stop=i == len(srcs) - 1)
                last.then_inc(done, 1)

            def broadcast(z, dst, src):
                n = src.shape[-1]
                pe.wait_ge(z["diag"], n // P)
                for a in range(0, n, HALF):
                    b = min(a + HALF, n)
                    last = nc.tensor.matmul(dst[:, a:b], ones[:, :], src[:, a:b], start=True, stop=True)
                last.then_inc(z["bc"], 1)

            def low_of(z, shared):
                if not shared:
                    return lambda k: (z["lo_v"], k + 1)
                return lambda k: (z["lo_p"] if k % 2 else z["lo_v"], k // 2 + 1)

            pe.wait_ge(consts, 5)
            def variance1(p):
                squares = n1_sq[p % 2]
                variance(bank(6 + p % 2), [((n1[p]["sum"], 5 if p == 0 else KT - 1), squares[0])], n1[p]["var"], PART // P)

            def broadcast1(p):
                if p >= 2:
                    pe.wait_ge(n1[p - 2]["val"], KT)
                broadcast(n1[p], bank(4 + p % 2, 0, PART), n1_diag[p])

            def keep_busy(n):
                for _ in range(n):
                    nc.tensor.matmul(bank(0, 0, P), ones[:, :], ident[:, :], start=True, stop=True)

            keep_busy(24)
            variance1(0)
            keep_busy(3)
            broadcast1(0)
            keep_busy(3)
            for p in range(PARTS):
                between = {}
                if p + 1 < PARTS:
                    between[6 if p == 0 else 1] = lambda: variance1(p + 1)
                    if p:
                        between[4] = lambda: broadcast1(p + 1)
                pair_part(0, 0, *part(p), low_of(n1[p], p >= 2), w_used if p + 1 == PARTS else None,
                          s1_half if p == 1 else None, between)
                if p == 0:
                    broadcast1(1)

            def through_slot1(kind_n, s, turn):
                pe.wait_ge(w_split, kind_n + 1)
                for h in range(2):
                    wait(pe, s1_out, 2 * turn + h - 1)
                    last = half_tile(s, slot(1, *span(h)), h, h_hi, h_lo)
                    last.then_inc(w_used if h else s1_half, 1)

            def value(c, n, s):
                wait(pe, val_out, c)
                project(n, s, 0, h_hi, h_lo)

            def pool_map(g, turn):
                pe.wait_ge(pw_lo_done, g + 1)
                pe.wait_ge(p_lo, 2 * (g + 1))
                for m in range(2):
                    for h in range(2):
                        pe.wait_ge(s1_out, 2 * (turn + m) + h - 1)
                        for k in range(2):
                            c = (2 * k + m) * P
                            last = three(slot(1, *span(h)), pw_hi[g % 2][:, c:c + P], pw_lo[g % 2][:, c:c + P],
                                         pp_hi[k][:, h * HALF:(h + 1) * HALF], pp_lo[k][:, h * HALF:(h + 1) * HALF],
                                         k == 0, k == 1)
                        last.then_inc(pool_mm if h else s1_half, 1)

            for kind, i in START[2:]:
                if kind == "m":
                    pool_map(i, TURN[kind, i])
                elif kind == "v":
                    value(i, CHUNK[kind, i], CHUNK[kind, i] % 2)
                else:
                    through_slot1(CHUNK[kind, i], CHUNK[kind, i] % 2, TURN[kind, i])
            def gate_pairs(c0, c1):
                with pe.Fori(c0, c1) as c:
                    for j in range(2):
                        through_slot1(2 * c + N_PAIRS + j, j, 2 * c + T_PAIRS + j)

            gate_pairs(PAIR0, MEAN_AT)
            for h in range(2):
                mean_of(slot(2, *span(h)), csum[:, h * HALF:(h + 1) * HALF], (cs_done, KT), ln["mean"])
            gate_pairs(MEAN_AT, MEAN_AT + 1)
            variance(slot(3), [((ln["sum"], KT), csum)], ln["var"], KT)
            through_slot1(2 * (MEAN_AT + 1) + N_PAIRS, 0, 2 * (MEAN_AT + 1) + T_PAIRS)
            broadcast(ln, slot(2), diag)
            through_slot1(2 * (MEAN_AT + 1) + N_PAIRS + 1, 1, 2 * (MEAN_AT + 1) + T_PAIRS + 1)
            gate_pairs(MEAN_AT + 2, KT)

            def pairs(first_n, free, read_out, mov_hi, mov_lo, ready, last_half=None):
                def two(i):
                    for j in range(2):
                        if isinstance(i, int) and i == 0:
                            pe.wait_ge(*free[j])
                        else:
                            pe.wait_ge(read_out, 2 * i + j - 1)
                        project(first_n + 2 * i + j, j, j, mov_hi, mov_lo,
                                ready if isinstance(i, int) and i == 0 and j == 0 else None,
                                last_half if isinstance(i, int) and i and j else None)
                two(0)
                n = KT // 2 - (last_half is not None)
                with pe.Fori(1, n) as i:
                    two(i)
                if last_half is not None:
                    two(KT // 2 - 1)

            pairs(N_OUT, ((val_out, KT), (s1_out, out_of(TURN["b", KT - 1]))), co_a, h_hi, h_lo, lambda h, k: (z_lo, h * KT + k + 1))
            pairs(N_MIX, ((co_a, KT - 1), (co_a, KT)), x1_done, cv_r, ga_r, lambda h, k: (co_lo, k + 1), mix_half)
            def variance2(h):
                variance(slot(3, *span(h)), [((n2_sum, KT + h), csum[:, h * HALF:(h + 1) * HALF])], n2[h]["var"])

            def broadcast2(h):
                broadcast(n2[h], slot(2, *span(h)), diag[:, h * HALF:(h + 1) * HALF])

            variance2(0)
            keep_busy(6)
            broadcast2(0)
            variance2(1)
            keep_busy(8)

            def up(p, s, n, dn):
                wait(pe, f_cb, p - 1)
                for j in range(2):
                    if dn is not None:
                        pe.wait_ge(dn_ev, dn + 2 * s + j)
                    project(n + j, j, 2 * s + j, h_hi, h_lo)

            def down(q, n, gs):
                pe.wait_ge(f_lo, 2 * q + 2)
                for m in range(KT):
                    if m % 4 == 0:
                        pe.wait_ge(w_split, n + m // 4 + 1)
                    if m < 4:
                        pe.wait_ge(f_cb, 2 * q + 3 + m // 2)
                    else:
                        pe.wait_ge(dn_ev, 8 * q + m - 3)
                    for h in range(2):
                        last = down_part(slot(m % 4, *span(h)), m, *span(h), gs)
                    last.then_inc(w_used if m % 4 == 3 else dn_mm, 1)

            def down_part(out, m, a, b, gs):
                for k in range(2):
                    c = (m // 4) * CH + ((m % 4) * 2 + k) * P
                    last = three(out, w_hi[:, c:c + P], w_lo[:, c:c + P],
                                 tile(cv_r, gs + k, a, b), tile(ga_r, gs + k, a, b), k == 0, k == 1)
                return last

            for h in range(2):
                pair_part(N_FFN, 0, *span(h), low_of(n2[h], True), w_used if h else None,
                          between={} if h else {2: lambda: broadcast2(1)})
            up(1, 1, N_FFN + 2, None)

            def ffn(i):
                n = N_FFN + UPC + 12 * i
                for s in range(2):
                    up(4 * i + 2 + s, s, n + 2 * s, None if isinstance(i, int) else 16 * i - 3)
                down(2 * i, n + 4, 0)
                for s in range(2):
                    up(4 * i + 4 + s, s, n + 6 + 2 * s, 16 * i + 5)
                down(2 * i + 1, n + 10, 2)
            ffn(0)
            with pe.Fori(1, STEPS // 2) as i:
                ffn(i)

            q, n = STEPS - 1, NCHUNKS - 2
            pe.wait_ge(f_lo, 2 * q + 2)
            pe.wait_ge(dn_ev, 8 * q)

            def final_variance(f):
                n = FINAL[f][1] - FINAL[f][0]
                variance(bank(6, 4 * f, 4 * f + 4), [((nf[f]["sum"], KT - 1), nf_sum[f % 2])], nf[f]["var"], n // P)

            def final_broadcast(f, dst):
                broadcast(nf[f], bank(dst, 0, FINAL[f][1] - FINAL[f][0]), nf_diag[f])

            for f, (a, b) in enumerate(FINAL):
                for m in range(KT):
                    t = f * KT + m
                    if m % 4 == 0:
                        pe.wait_ge(w_split, n + m // 4 + 1)
                    wait(pe, x2_done, t - 5)
                    down_part(bank(t % 6, 0, b - a), m, a, b, 0).then_inc(x2_mm, 1)
                    if f and m == STATS_AT[f]:
                        final_variance(f - 1)
                    if f == 2 and m == 0:
                        final_broadcast(0, 7)
            pe.wait_ge(x2_done, 2 * KT + 6)
            for f, dst in ((1, 0), (1, 1)):
                final_broadcast(f, dst)
            final_variance(2)
            for f, dst in ((2, 2), (2, 3)):
                final_broadcast(f, dst)


def lay_out(np, x, w_in, b_in, conv_dw_w, conv_dw_b, conv_ln_g, conv_ln_b, conv_w_out, pool_w, pool_scale,
            mix_w_out, norm_mix, ffn_w_up, ffn_dw_w, ffn_dw_b, ffn_w_down, norm_ffn, norm_final):
    def block_tiles(w):
        k, n = w.shape
        return w.reshape(k // P, P, n // P, P).transpose(2, 1, 0, 3).reshape(n // P, P, k)

    parts = {kind: block_tiles(w_in[0][:, i * DM:(i + 1) * DM]) for kind, i in _part.items()}
    chunks = [parts[kind][i] for kind, i in in_order() if kind != "m"]
    chunks += list(block_tiles(conv_w_out[0])) + list(block_tiles(mix_w_out[0]))
    up = block_tiles(ffn_w_up[0])
    dn = ffn_w_down[0].reshape(STEPS, CHUNK_PAIRS, P, 2, 4, P).transpose(0, 3, 2, 4, 1, 5).reshape(STEPS, 2, P, CH)

    def ups(q):
        return [t for p in range(CHUNK_PAIRS * q, CHUNK_PAIRS * (q + 1)) for t in (up[p], up[p + FT])]

    chunks += ups(0)
    for q in range(1, STEPS):
        chunks += ups(q) + list(dn[q - 1])
    chunks += list(dn[STEPS - 1])
    stream = np.ascontiguousarray(np.concatenate(chunks, axis=0))

    def per_channel(v):
        return v.reshape(-1, P).T

    edge = np.zeros((NG, WPAD), np.float32)
    for g, w in enumerate(WINDOWS):
        edge[g] = w / np.minimum(np.arange(1, WPAD + 1), w)
    params = np.ascontiguousarray(np.concatenate([
        per_channel(norm_mix[0]), per_channel(b_in[0]),
        conv_dw_w[0].reshape(TAPS, KT, P).transpose(2, 1, 0).reshape(P, KT * TAPS),
        per_channel(conv_dw_b[0]), per_channel(conv_ln_g[0]), per_channel(conv_ln_b[0]), per_channel(pool_scale[0]),
        per_channel(norm_ffn[0]), per_channel(norm_final),
        ffn_dw_w[0].reshape(3, 2 * FT, P).transpose(2, 1, 0).reshape(P, 2 * FT * 3),
        per_channel(ffn_dw_b[0]), np.broadcast_to(edge.reshape(1, -1), (P, NG * WPAD)),
    ], axis=1))
    pw = np.ascontiguousarray(pool_w[0].reshape(NG, 2, P, 2, P).transpose(2, 0, 1, 3, 4).reshape(P, 2 * CH))
    return {"xT": np.ascontiguousarray(x[0].T), "wstream": stream, "pool_w": pw, "params": params}


def kernel(**inputs):
    import numpy as np
    import concourse.bacc as bacc
    from concourse import mybir
    from concourse.bass_utils import run_bass_kernel_spmd

    arrays = lay_out(np, **{k: np.asarray(v) for k, v in inputs.items()})
    nc = bacc.Bacc("TRN2", target_bir_lowering=False, num_devices=1)
    args = [nc.dram_tensor(f"in_{n}", arrays[n].shape, mybir.dt.float32, kind="ExternalInput").ap()
            for n in ("xT", "wstream", "pool_w", "params")]
    out = nc.dram_tensor("outT", (DM, SEQ), mybir.dt.float32, kind="ExternalOutput").ap()
    build(nc, *args, out)
    r = run_bass_kernel_spmd(nc, [{f"in_{n}": a for n, a in arrays.items()}], core_ids=[0])
    return np.ascontiguousarray(r.results[0]["outT"].T)[None]
```
